# Optimizing a Trainium2 kernel written in Bass

```python
import jax, jax.numpy as jnp
from jax import lax
import numpy as np

D_MODEL = 1024
BATCH = 1
SEQ = 512
DEPTH = 2

CTX_LEN = 256
GRID_W = 64
HEAD_DIM = 64
A_HEADS = 8
A_KV_HEADS = 2
A_WINDOW = 128
A_BLOCK = 128
B_HEADS = 8
NA_ROWS = 8
NA_COLS = 16
C_CH = 512
C_KSIZE = 31
M_HEADS = 4
M_DIM = 128
M_CHUNK = 128
N_BRANCH = 4
BRANCH_W = 512
N_EXPERTS = 16
EXPERT_FF = 1024
CAPACITY_FACTOR = 2
ROPE_BASE = 10000.0
LN_EPS = 1e-6
NEG_INF = -1e30

PROJ_SIZES = (A_HEADS * HEAD_DIM, A_KV_HEADS * HEAD_DIM, A_KV_HEADS * HEAD_DIM,
              B_HEADS * HEAD_DIM, B_HEADS * HEAD_DIM, B_HEADS * HEAD_DIM,
              2 * C_CH,
              M_HEADS * M_DIM, M_HEADS * M_DIM, M_HEADS * M_DIM, M_HEADS * M_DIM, 4 * M_HEADS)
PROJ_W = sum(PROJ_SIZES)

kernel_name = 'hybrid_dit_parallel_mixers_ec_moe'

def _layer_norm(x, g=None, b=None):
    xf = x.astype(jnp.float32)
    mu = xf.mean(-1, keepdims=True)
    var = jnp.square(xf - mu).mean(-1, keepdims=True)
    y = (xf - mu) * lax.rsqrt(var + LN_EPS)
    if g is not None:
        y = y * g.astype(jnp.float32) + b.astype(jnp.float32)
    return y.astype(x.dtype)

def _split_proj(p):
    out, off = [], 0
    for n in PROJ_SIZES:
        out.append(p[..., off:off + n])
        off += n
    return out

def _heads(t, h):
    return t.reshape(t.shape[:2] + (h, -1))

def _axial_rope(x):
    T = x.shape[1]
    t = jnp.arange(T)
    half = HEAD_DIM // 2
    nf = half // 2
    inv = ROPE_BASE ** (-jnp.arange(nf, dtype=jnp.float32) / nf)

    def rot(xa, pos):
        ang = pos.astype(jnp.float32)[:, None] * inv[None, :]
        cos = jnp.cos(ang)[:, None, :].astype(x.dtype)
        sin = jnp.sin(ang)[:, None, :].astype(x.dtype)
        x1, x2 = xa[..., :nf], xa[..., nf:]
        return jnp.concatenate([x1 * cos - x2 * sin, x1 * sin + x2 * cos], axis=-1)

    return jnp.concatenate([rot(x[..., :half], t // GRID_W), rot(x[..., half:], t % GRID_W)], axis=-1)

def _windowed_gqa(q, k, v, kc, vc, sink):
    B, S = q.shape[:2]
    L = kc.shape[1]
    G = A_HEADS // A_KV_HEADS
    nb = S // A_BLOCK
    nk = 3 * A_BLOCK
    qb = q.reshape(B, nb, A_BLOCK, A_KV_HEADS, G, HEAD_DIM) * HEAD_DIM ** -0.5

    def band(t):
        tp = jnp.pad(t, ((0, 0), (A_BLOCK, A_BLOCK), (0, 0), (0, 0)))
        tp = tp.reshape(B, nb + 2, A_BLOCK, A_KV_HEADS, HEAD_DIM)
        return jnp.concatenate([tp[:, :-2], tp[:, 1:-1], tp[:, 2:]], axis=2)

    kb, vb = band(k), band(v)
    rel = jnp.arange(nk)[None, :] - jnp.arange(A_BLOCK)[:, None] - A_BLOCK
    in_band = jnp.abs(rel) <= A_WINDOW
    kpos = jnp.arange(nb)[:, None] * A_BLOCK - A_BLOCK + jnp.arange(nk)[None, :]
    in_seq = (kpos >= 0) & (kpos < S)
    mask = in_band[None] & in_seq[:, None, :]
    s_loc = jnp.einsum('bnqgrd,bnkgd->bngrqk', qb, kb).astype(jnp.float32)
    s_loc = jnp.where(mask[None, :, None, None], s_loc, NEG_INF)
    s_ctx = jnp.einsum('bnqgrd,bkgd->bngrqk', qb, kc).astype(jnp.float32)
    s_sink = jnp.broadcast_to(sink.astype(jnp.float32).reshape(1, 1, A_KV_HEADS, G, 1, 1), s_ctx.shape[:-1] + (1,))
    p = jax.nn.softmax(jnp.concatenate([s_loc, s_ctx, s_sink], axis=-1), axis=-1).astype(v.dtype)
    o = (jnp.einsum('bngrqk,bnkgd->bnqgrd', p[..., :nk], vb)
         + jnp.einsum('bngrqk,bkgd->bnqgrd', p[..., nk:nk + L], vc))
    return o.reshape(B, S, A_HEADS * HEAD_DIM)

def _ctx_attention(q, k, v, sink=None):
    B, L, H, hd = q.shape
    KV = k.shape[2]
    G = H // KV
    qg = q.reshape(B, L, KV, G, hd) * hd ** -0.5
    s = jnp.einsum('bqgrd,bkgd->bgrqk', qg, k).astype(jnp.float32)
    if sink is not None:
        s = jnp.concatenate([s, jnp.broadcast_to(sink.astype(jnp.float32).reshape(1, KV, G, 1, 1), s.shape[:-1] + (1,))], axis=-1)
    p = jax.nn.softmax(s, axis=-1)[..., :L].astype(v.dtype)
    o = jnp.einsum('bgrqk,bkgd->bqgrd', p, v)
    return o.reshape(B, L, H * hd)

def _neighborhood_attn(q, k, v, kc, vc, rpb):
    B, T, H, hd = q.shape
    rows = T // GRID_W
    wh = min(NA_ROWS, rows)
    grid = lambda t: t.reshape(B, rows, GRID_W, H, hd)
    qg = grid(q) * hd ** -0.5
    r = jnp.arange(rows)
    row_idx = jnp.clip(r - wh // 2, 0, rows - wh)[:, None] + jnp.arange(wh)[None, :]
    kg = grid(k)[:, row_idx]
    vg = grid(v)[:, row_idx]
    col = jnp.arange(GRID_W)
    c0 = jnp.clip(col - NA_COLS // 2, 0, GRID_W - NA_COLS)
    col_ok = (col[None, :] >= c0[:, None]) & (col[None, :] < c0[:, None] + NA_COLS)
    dr = row_idx - r[:, None] + NA_ROWS - 1
    dc = jnp.clip(col[None, :] - col[:, None] + NA_COLS - 1, 0, 2 * NA_COLS - 2)
    bias = rpb[:, dr[:, :, None, None], dc[None, None]].transpose(1, 0, 3, 2, 4)
    s_nb = jnp.einsum('brqhd,brwkhd->brhqwk', qg, kg).astype(jnp.float32) + bias.astype(jnp.float32)
    s_nb = jnp.where(col_ok[:, None, :], s_nb, NEG_INF).reshape(B, rows, H, GRID_W, wh * GRID_W)
    s_ctx = jnp.einsum('brqhd,bkhd->brhqk', qg, kc).astype(jnp.float32)
    p = jax.nn.softmax(jnp.concatenate([s_nb, s_ctx], axis=-1), axis=-1).astype(v.dtype)
    nk = wh * GRID_W
    o = (jnp.einsum('brhqwk,brwkhd->brqhd', p[..., :nk].reshape(B, rows, H, GRID_W, wh, GRID_W), vg)
         + jnp.einsum('brhqk,bkhd->brqhd', p[..., nk:], vc))
    return o.reshape(B, T, H * hd)

def _conformer_conv(u, w_dw, b_dw, g, b):
    a, gate = jnp.split(u, 2, axis=-1)
    y = a * jax.nn.sigmoid(gate)
    y = lax.conv_general_dilated(y, w_dw[:, None, :].astype(y.dtype), (1,), [(C_KSIZE // 2, C_KSIZE // 2)],
                                 dimension_numbers=('NWC', 'WIO', 'NWC'), feature_group_count=C_CH) + b_dw
    return jax.nn.silu(_layer_norm(y, g, b))

def _mlstm_chunk(carry, inp):
    C, n, m = carry
    q, k, v, ig, lf = inp
    Lc = q.shape[-2]
    F = jnp.cumsum(lf, axis=-1)
    a = F + m[..., None]
    causal = jnp.tril(jnp.ones((Lc, Lc), dtype=bool))
    logw = jnp.where(causal, F[..., :, None] - F[..., None, :] + ig[..., None, :], -jnp.inf)
    mt = jnp.maximum(a, logw.max(-1))
    w_inter = jnp.exp(a - mt)
    s = jnp.einsum('bhtd,bhsd->bhts', q, k) * jnp.exp(logw - mt[..., None])
    num = w_inter[..., None] * jnp.einsum('bhtd,bhde->bhte', q, C) + jnp.einsum('bhts,bhse->bhte', s, v)
    den = w_inter * jnp.einsum('bhtd,bhd->bht', q, n) + s.sum(-1)
    h = num / jnp.maximum(jnp.abs(den), jnp.exp(-mt))[..., None]
    FL = F[..., -1]
    g = FL[..., None] - F + ig
    m_new = jnp.maximum(FL + m, g.max(-1))
    decay = jnp.exp(FL + m - m_new)
    w = jnp.exp(g - m_new[..., None])
    C_new = decay[..., None, None] * C + jnp.einsum('bhs,bhsd,bhse->bhde', w, k, v)
    n_new = decay[..., None] * n + jnp.einsum('bhs,bhsd->bhd', w, k)
    return (C_new, n_new, m_new), h

def _mlstm_scan(q, k, v, ig, lf, state):
    B, H, T, d = q.shape
    nc = T // M_CHUNK
    chunks = lambda t: jnp.moveaxis(t.reshape(t.shape[:2] + (nc, M_CHUNK) + t.shape[3:]), 2, 0)
    state, h = lax.scan(_mlstm_chunk, state, (chunks(q), chunks(k), chunks(v), chunks(ig), chunks(lf)))
    return jnp.moveaxis(h, 0, 2).reshape(B, H, T, d), state

def _mlstm_inputs(q, k, v, gates, gate_b):
    B, T, _ = q.shape
    heads = lambda t: t.astype(jnp.float32).reshape(B, T, M_HEADS, M_DIM).transpose(0, 2, 1, 3)
    g = (gates.astype(jnp.float32) + gate_b.astype(jnp.float32)).reshape(B, T, 4, M_HEADS).transpose(2, 0, 3, 1)
    fwd = (g[0], jax.nn.log_sigmoid(g[1]))
    bwd = (g[2], jax.nn.log_sigmoid(g[3]))
    return heads(q), heads(k) * M_DIM ** -0.5, heads(v), fwd, bwd

def _bi_mlstm(lat, ctx, gate_b, need_ctx_out):
    ql, kl, vl, fl, bl = _mlstm_inputs(lat[0], lat[1], lat[2], lat[4], gate_b)
    qc, kc, vc, fc, bc = _mlstm_inputs(ctx[0], ctx[1], ctx[2], ctx[4], gate_b)
    B = ql.shape[0]
    zero = (jnp.zeros((B, M_HEADS, M_DIM, M_DIM), jnp.float32), jnp.zeros((B, M_HEADS, M_DIM), jnp.float32),
            jnp.zeros((B, M_HEADS), jnp.float32))
    rev = lambda t: jnp.flip(t, axis=2)
    hcf, st_f = _mlstm_scan(qc, kc, vc, fc[0], fc[1], zero)
    hcb, st_b = _mlstm_scan(rev(qc), rev(kc), rev(vc), rev(bc[0]), rev(bc[1]), zero)
    hlf, _ = _mlstm_scan(ql, kl, vl, fl[0], fl[1], st_f)
    hlb, _ = _mlstm_scan(rev(ql), rev(kl), rev(vl), rev(bl[0]), rev(bl[1]), st_b)

    def out(hf, hb, o_pre):
        Bb, H, T, d = hf.shape
        h = (hf + rev(hb)).transpose(0, 2, 1, 3).reshape(Bb, T, H * d)
        return (jax.nn.sigmoid(o_pre.astype(jnp.float32)) * h).astype(o_pre.dtype)

    y_lat = out(hlf, hlb, lat[3])
    y_ctx = out(hcf, hcb, ctx[3]) if need_ctx_out else None
    return y_lat, y_ctx

def _merge(h, ys, w_branch, w_gate, b_gate, w_out):
    g = jax.nn.sigmoid((h @ w_gate + b_gate).astype(jnp.float32)).astype(h.dtype)
    z = g[..., :D_MODEL] * (ys[0] @ w_branch[0])
    for i in range(1, N_BRANCH):
        z = z + g[..., i * D_MODEL:(i + 1) * D_MODEL] * (ys[i] @ w_branch[i])
    return z @ w_out

def _token_mixing(hl, hc, need_ctx, w_in, sink, rpb, conv_w, conv_b, conv_g, conv_bb, gate_b,
                  w_branch, w_gate, b_gate, w_out):
    pl = _split_proj(hl @ w_in)
    pc = _split_proj(hc @ w_in)
    kac, vac = _heads(pc[1], A_KV_HEADS), _heads(pc[2], A_KV_HEADS)
    ya = _windowed_gqa(_axial_rope(_heads(pl[0], A_HEADS)), _axial_rope(_heads(pl[1], A_KV_HEADS)),
                       _heads(pl[2], A_KV_HEADS), kac, vac, sink)
    kbc, vbc = _heads(pc[4], B_HEADS), _heads(pc[5], B_HEADS)
    yb = _neighborhood_attn(_heads(pl[3], B_HEADS), _heads(pl[4], B_HEADS), _heads(pl[5], B_HEADS), kbc, vbc, rpb)
    yc = _conformer_conv(pl[6], conv_w, conv_b, conv_g, conv_bb)
    yd, yd_c = _bi_mlstm(pl[7:12], pc[7:12], gate_b, need_ctx)
    out_lat = _merge(hl, (ya, yb, yc, yd), w_branch, w_gate, b_gate, w_out)
    out_ctx = None
    if need_ctx:
        ya_c = _ctx_attention(_heads(pc[0], A_HEADS), kac, vac, sink)
        yb_c = _ctx_attention(_heads(pc[3], B_HEADS), kbc, vbc)
        yc_c = _conformer_conv(pc[6], conv_w, conv_b, conv_g, conv_bb)
        out_ctx = _merge(hc, (ya_c, yb_c, yc_c, yd_c), w_branch, w_gate, b_gate, w_out)
    return out_lat, out_ctx

def _expert_choice_ffn(h, w_router, w1, w3, w2):
    B, T, D = h.shape
    cap = CAPACITY_FACTOR * T // N_EXPERTS
    aff = jax.nn.softmax((h @ w_router).astype(jnp.float32), axis=-1)
    vals, idx = lax.top_k(aff.transpose(0, 2, 1), cap)
    xg = jax.vmap(lambda hb, ib: hb[ib])(h, idx)
    hid = jax.nn.silu(jnp.einsum('becd,edf->becf', xg, w1)) * jnp.einsum('becd,edf->becf', xg, w3)
    y = jnp.einsum('becf,efd->becd', hid, w2) * vals[..., None].astype(h.dtype)
    return jax.vmap(lambda yb, ib: jnp.zeros((T, D), h.dtype).at[ib.reshape(-1)].add(yb.reshape(-1, D)))(y, idx)

def setup_inputs(seed: int = 0) -> dict:
    key = jax.random.key(seed)
    ks = jax.random.split(key, 40)
    f32 = jnp.float32
    D = D_MODEL
    beta = (8.0 * DEPTH) ** -0.25
    nrm = lambda k, shape, s: jax.random.normal(k, shape, f32) * s
    f_bias = jnp.linspace(3.0, 6.0, M_HEADS, dtype=f32)[None, :]
    mlstm_gate_b = jnp.concatenate([nrm(ks[10], (DEPTH, M_HEADS), 0.1), f_bias + nrm(ks[11], (DEPTH, M_HEADS), 0.1),
                                    nrm(ks[12], (DEPTH, M_HEADS), 0.1), f_bias + nrm(ks[13], (DEPTH, M_HEADS), 0.1)], axis=-1)
    return {
        'x': nrm(ks[0], (BATCH, SEQ, D), 1.0),
        'c': nrm(ks[1], (BATCH, D), 1.0),
        'ctx': nrm(ks[2], (BATCH, CTX_LEN, D), 1.0),
        'c_ctx': nrm(ks[3], (D,), 1.0),
        'w_mod': nrm(ks[4], (DEPTH, D, 6 * D), 0.5 * D ** -0.5),
        'b_mod': nrm(ks[5], (DEPTH, 6 * D), 0.02),
        'w_in': nrm(ks[6], (DEPTH, D, PROJ_W), D ** -0.5),
        'attn_sink': nrm(ks[7], (DEPTH, A_HEADS), 0.5),
        'na_rpb': nrm(ks[8], (DEPTH, B_HEADS, 2 * NA_ROWS - 1, 2 * NA_COLS - 1), 0.1),
        'conv_w': nrm(ks[9], (DEPTH, C_KSIZE, C_CH), C_KSIZE ** -0.5),
        'conv_b': nrm(ks[14], (DEPTH, C_CH), 0.02),
        'conv_ln_g': 1.0 + nrm(ks[15], (DEPTH, C_CH), 0.02),
        'conv_ln_b': nrm(ks[16], (DEPTH, C_CH), 0.02),
        'mlstm_gate_b': mlstm_gate_b,
        'w_branch': nrm(ks[17], (DEPTH, N_BRANCH, BRANCH_W, D), beta * BRANCH_W ** -0.5),
        'w_gate': nrm(ks[18], (DEPTH, D, N_BRANCH * D), D ** -0.5),
        'b_gate': nrm(ks[19], (DEPTH, N_BRANCH * D), 0.02),
        'w_out': nrm(ks[20], (DEPTH, D, D), beta * D ** -0.5),
        'ln1_g': 1.0 + nrm(ks[21], (DEPTH, D), 0.02),
        'ln1_b': nrm(ks[22], (DEPTH, D), 0.02),
        'w_router': nrm(ks[23], (DEPTH, D, N_EXPERTS), D ** -0.5),
        'w_exp_gate': nrm(ks[24], (DEPTH, N_EXPERTS, D, EXPERT_FF), D ** -0.5),
        'w_exp_up': nrm(ks[25], (DEPTH, N_EXPERTS, D, EXPERT_FF), D ** -0.5),
        'w_exp_down': nrm(ks[26], (DEPTH, N_EXPERTS, EXPERT_FF, D), beta * EXPERT_FF ** -0.5),
        'ln2_g': 1.0 + nrm(ks[27], (DEPTH, D), 0.02),
        'ln2_b': nrm(ks[28], (DEPTH, D), 0.02),
    }

def reference(x, c, ctx, c_ctx, w_mod, b_mod, w_in, attn_sink, na_rpb, conv_w, conv_b, conv_ln_g, conv_ln_b,
              mlstm_gate_b, w_branch, w_gate, b_gate, w_out, ln1_g, ln1_b, w_router, w_exp_gate, w_exp_up,
              w_exp_down, ln2_g, ln2_b):
    alpha = (2.0 * DEPTH) ** 0.25
    xl, xc = x, ctx
    s_lat = jax.nn.silu(c)
    s_ctx = jax.nn.silu(c_ctx)
    for l in range(DEPTH):
        need_ctx = l < DEPTH - 1
        mod_l = (s_lat @ w_mod[l] + b_mod[l])[:, None, :]
        mod_c = s_ctx @ w_mod[l] + b_mod[l]
        sh1, sc1, g1, sh2, sc2, g2 = jnp.split(mod_l, 6, axis=-1)
        csh1, csc1, cg1, csh2, csc2, cg2 = jnp.split(mod_c, 6, axis=-1)
        hl = _layer_norm(xl) * (1.0 + sc1) + sh1
        hc = _layer_norm(xc) * (1.0 + csc1) + csh1
        yl, yc = _token_mixing(hl, hc, need_ctx, w_in[l], attn_sink[l], na_rpb[l], conv_w[l], conv_b[l],
                               conv_ln_g[l], conv_ln_b[l], mlstm_gate_b[l], w_branch[l], w_gate[l], b_gate[l], w_out[l])
        xl = _layer_norm(alpha * xl + g1 * yl, ln1_g[l], ln1_b[l])
        if need_ctx:
            xc = _layer_norm(alpha * xc + cg1 * yc, ln1_g[l], ln1_b[l])
        hl = _layer_norm(xl) * (1.0 + sc2) + sh2
        ml = _expert_choice_ffn(hl, w_router[l], w_exp_gate[l], w_exp_up[l], w_exp_down[l])
        xl = _layer_norm(alpha * xl + g2 * ml, ln2_g[l], ln2_b[l])
        if need_ctx:
            hc = _layer_norm(xc) * (1.0 + csc2) + csh2
            mc = _expert_choice_ffn(hc, w_router[l], w_exp_gate[l], w_exp_up[l], w_exp_down[l])
            xc = _layer_norm(alpha * xc + cg2 * mc, ln2_g[l], ln2_b[l])
    return xl


_drawn_inputs = setup_inputs


def setup_inputs(seed=0):
    import zlib

    import numpy as np

    out = dict(_drawn_inputs(seed))
    spreads = {}
    factors = {'attn_sink': 64.0,
     'na_rpb': 64.0,
     'conv_b': 8.0,
     'conv_ln_g': 24.61,
     'conv_ln_b': 24.16,
     'b_gate': 8.0}
    for name, (base, spread) in spreads.items():
        noise = np.random.default_rng([zlib.crc32(name.encode()), seed]).standard_normal(out[name].shape)
        drawn = base * np.exp(spread * noise) if base else spread * noise
        out[name] = __import__('jax').numpy.asarray(drawn.astype(out[name].dtype))
    for name, factor in factors.items():
        out[name] = (out[name] * factor).astype(out[name].dtype)
    return out
```

```python
import concourse.bass as bass
from concourse import mybir
from contextlib import ExitStack, contextmanager
import numpy as np

P = 128
D = 1024
KD = D // P
DEPTH = 2
LAT, CTX = 512, 256
TOK = LAT + CTX
TL, TC = LAT // P, CTX // P
NT = TL + TC
GRID_W = 64
HD = 64
HEADS = 8
MH = 4
MU = 2 * MH
KS = 31
HALO = KS // 2
BW = 512
FB = BW // P
NBR = 4
E = 16
CAPL, CAPC = 2 * LAT // E, 2 * CTX // E
CAP = CAPL + CAPC
EPS = 1e-6
NEG = -1e30
ALPHA = float((2.0 * DEPTH) ** 0.25)
QSCALE = float(HD ** -0.5)
MSCALE = float(P ** -0.5)
RING = 4
NCH = 512
DROWS = 16
LSEG, CSEG = LAT + 2 * HALO, CTX + 2 * HALO
WORK = 16500
MV = P + 1

MOD_BLOCKS = 6 * D // NCH
IN_BLOCKS = 11
B_IN = MOD_BLOCKS
B_MERGE = B_IN + IN_BLOCKS
B_OUT = B_MERGE + 2 * 2 * NBR
B_EXP = B_OUT + 2
LAYER_BLOCKS = B_EXP + 6 * E


LAYER_SIGNALS = """
conv_part merge_part out_part mod_bias_in params_in mod_row mod_out xhat x_in0 x_in1 conv_zero rope_in
bias_in0 bias_in1 a_rcp a_scaled a_max rows1_in x1_in router_in slots slots_out rows2_in acc_zero e_put
pair_in xg x2 x_out mod_cols h_done xhat_T conv_glu ab_out rope_done rope_rot conv_sum conv_sq conv_sumsq
a_exp a_scores a_probT a_turned a_out a_values d_out m_cum m_diag m_rows m_scores m_arg m_keys m_weights m_num
m_mm m_kw m_state m_outer o_sig o_mm o_gated o_out o_turned z_part p_y xn h2_done xn_T r_logits r_aff r_affT
r_slotT g_out g_mm e_acc e_hid e_turned e_hidT e_y e_comb var std conv_sig conv_cent conv_var conv_std
conv_normed m_abs m_log m_exps m_arg2 m_gate m_carried z_gate p_var p_std r_cent r_exp e_sil q_var q_std
ab_part d_part
""".split()


def tiles_out(l):
    return NT if l < DEPTH - 1 else TL


def units(l):
    return [(kind, h, n) for kind in "AB" for h in range(HEADS) for n in range(tiles_out(l))]


def local_keys(kind, n):
    if n >= TL:
        return 0, 0
    if kind == "B":
        return 0, LAT
    return max(n - 1, 0) * P, min(n + 2, TL) * P


class Chain:

    def __init__(self, eng, sem):
        self.eng, self.sem, self.n, self.at = eng, sem, 0, None

    def __call__(self, ins):
        self.n += 1
        ins.then_inc(self.sem, 1)

    def wait(self, lag=0):
        self.eng.wait_ge(self.sem, self.n - lag if self.at is None else self.at + self.n - lag)


class Signal:
    turns = 1

    def __init__(self, sem):
        self.sem, self.before, self.now = sem, 0, 0

    def by(self, k):
        self.now += k * Signal.turns
        return self.sem, k

    def at(self, v):
        return self.sem, v + self.before

    def next_layer(self):
        self.before, self.now = self.before + self.now, 0


@contextmanager
def turns(eng, n):
    Signal.turns = n
    with eng.Fori(0, n) as i:
        yield i
    Signal.turns = 1


class Parts:

    def __init__(self, sem, ring_used, layer, order, count):
        self.early, self.place, n = sem, {}, 0
        self.ring_used, self.first = ring_used, layer * LAYER_BLOCKS
        for b, j in order:
            last = j == (count[b] if isinstance(count, dict) else count) - 1
            n += not last
            self.place[b, j] = None if last else n

    def by(self, b, j):
        return (self.ring_used, 1) if self.place[b, j] is None else self.early.by(1)

    def of(self, b, j):
        n = self.place[b, j]
        return (self.ring_used, self.first + b + 1) if n is None else self.early.at(n)


def build(nc, A, out):
    f32 = mybir.dt.float32
    ALU = mybir.AluOpType
    ACT = mybir.ActivationFunctionType
    AX = mybir.AxisListType.X
    ctx = ExitStack()
    with ctx:
        def sb(name, shape):
            return ctx.enter_context(nc.sbuf_tensor(name, shape, f32))

        sems = {n: Signal(ctx.enter_context(nc.semaphore(n))) for n in LAYER_SIGNALS}
        for n in ("stage_done", "ring_used", "const_in", "silu", "act_own", "dve_own",
                  *(f"ring_in{i}" for i in range(RING))):
            sems[n] = ctx.enter_context(nc.semaphore(n))

        def S(name, l=None):
            assert (name in LAYER_SIGNALS) == (l is not None), name
            return sems[name]

        mod_d = nc.dram_tensor("mod_d", (DEPTH, 2, 6 * D), f32, kind="Internal").ap()
        x_d = nc.dram_tensor("x_d", (NT, P, D), f32, kind="Internal").ap()
        slot_d = nc.dram_tensor("slot_d", (DEPTH, 2, E, TOK), f32, kind="Internal").ap()

        ring = sb("ring", [P, RING, KD, NCH])
        hT = sb("hT", [P, KD * TOK])
        ys = sb("ys", [P, NBR * FB * TOK])
        work = sb("work", [P, WORK])
        consts = sb("consts", [P, 4 * P + 3 * P])
        s2T = sb("s2T", [P, KD, 2])
        iotas = sb("iotas", [P, 1 + CAPL])
        modc = sb("modc", [P, 4, KD, 2])
        conv_c = sb("conv_c", [P, FB, KS + 3])
        gate_b = sb("gate_b", [P, 4 * MH])
        mgate_b = sb("mgate_b", [P, NBR, KD])
        sink_b = sb("sink_b", [P, HEADS])
        ps = ctx.enter_context(nc.psum_tensor("ps", [P, 8, 512], f32))
        psf = ps[:, :, :].rearrange("p b n -> p (b n)")

        ident, ones, upper, lower = (consts[:, i * P:(i + 1) * P] for i in range(4))
        band = consts[:, 4 * P:7 * P]
        neg_ge, neg_le = band[:, 0:P], band[:, 2 * P:3 * P]
        slot_col, slot_row = iotas[:, 0:1], iotas[:, 1:1 + CAPL]

        def cut(t, at, *shape):
            n = int(np.prod(shape))
            assert at + n <= t.shape[1], (at, n, t.shape)
            v = t[:, at:at + n]
            if len(shape) == 2:
                v = v.rearrange("p (a b) -> p a b", a=shape[0])
            if len(shape) == 3:
                v = v.rearrange("p (a b c) -> p a b c", a=shape[0], b=shape[1])
            return v, at + n

        h_v, _ = cut(hT, 0, KD, TOK)
        acc, _ = cut(hT, 0, NT, D)
        pick_l, o = cut(hT, 0, TL, E, CAPL)
        pick_c, _ = cut(hT, o, TC, E, CAPC)
        y_v = [cut(ys, i * FB * TOK, FB, TOK)[0] for i in range(NBR)]
        mod_row, o = cut(ys, 0, 6 * D)
        mod_bias, _ = cut(work, 0, 6 * D)
        xin, o = cut(work, 0, 2, D)
        xhat, o = cut(work, o, 2, D)
        gates, o = cut(work, 0, NT, 4 * MH)
        kA, o = cut(work, o, 2, TOK)
        vA, o = cut(work, o, NT, P)
        kB, o = cut(work, o, FB, TOK)
        vB, o = cut(work, o, NT, BW)
        cpad, oc = cut(work, o, FB, LSEG + CSEG)
        csq, oc = cut(work, oc, 2, TOK)
        cstd, oc = cut(work, oc, TOK)
        csg = cstd
        rope_t, oc = cut(work, oc, 2, LAT)
        rot, oc = cut(work, oc, P)
        rope_s, oc = cut(work, oc, 2, LAT)
        bias, oc = cut(work, o, 2, DROWS * GRID_W)
        prob, oc = cut(work, oc, 3, TOK)
        probT, oc = cut(work, oc, 2, TOK)
        soft, oc = cut(work, oc, 4, 8)
        kD, o = cut(work, NT * 4 * MH, MH, TOK)
        vD, o = cut(work, o, NT, MH, MV)
        hD, o = cut(work, o, NT, BW)
        mA, o = cut(work, o, MU, P)
        mB, o = cut(work, o, MU, P)
        mC, o = cut(work, o, MU, MV)
        cst, o = cut(work, o, MU, MV)
        ig_c, o = cut(work, o, NT, MU)
        lf_c, o = cut(work, o, NT, MU)
        lt_c, o = cut(work, o, NT, MU)
        u_c, o = cut(work, o, NT, MU)
        F_c, o = cut(work, o, NT, MU)
        FL_c, o = cut(work, o, NT, MU)
        m_c, o = cut(work, o, MU)
        cm_c, o = cut(work, o, 2, MU)
        M_c, o = cut(work, o, 2, MU)
        nM_c, o = cut(work, o, MU)
        ex_in, o = cut(work, o, 4, MU)
        ex_c, o = cut(work, o, 4, MU)
        den, o = cut(work, o, 3, MU)
        sig_o, _ = cut(work, NT * 4 * MH, 2, BW)
        zT, _ = cut(work, WORK - KD * TOK, KD, TOK)
        mg_s, o = cut(work, 0, 2, TOK)
        mg_t, o = cut(work, o, 2, TOK)
        x1, oX = cut(work, 0, NT, D)
        xn, o = cut(ys, 0, NT * D)
        rows1, o = cut(ys, o, 4, D)
        t1, o = cut(ys, o, 2, D)
        aff, o = cut(work, oX, NT, E)
        slotT, o = cut(work, o, NT, E)
        wr, o = cut(work, o, KD, E)
        rsm, o = cut(work, o, 4, NT)
        affR, o = cut(work, o, TOK)
        left, o = cut(work, o, TOK)
        took, o = cut(work, o, TOK)
        slotR, o = cut(work, o, TOK)
        top8, o = cut(work, o, 8)
        xgA, _ = cut(ys, NT * D, KD // 2, E, CAP)
        xgB, _ = cut(work, WORK - KD * TOK, KD // 2, E, CAP)
        pair, o = cut(work, oX, 2, TOK)
        xg, o = cut(work, o, KD, CAP)
        hidT, o = cut(work, o, KD, CAP)
        ysb, o = cut(work, o, D)
        assert o <= WORK - KD * TOK
        rows2, o = cut(ys, 0, 4, D)
        hid, o = cut(ys, o, D)
        put, o = cut(ys, o, TOK)
        stat = sb("stat", [P, 2, 24])

        stage = S("stage_done")
        ring_in = [S(f"ring_in{i}") for i in range(RING)]
        ring_used = S("ring_used")

        def conv_parts(l):
            order = [(B_IN + b, j) for j in range(FB) for b in range(2)]
            return Parts(S("conv_part", l), ring_used, l, order, FB)

        def ab_groups(l):
            g = [(2, j, FB, "f", "qA") for j in range(FB)]
            g += [(3, j, 2 + NT, "f", "kA") for j in range(2)] + [(3, 2 + t, 2 + NT, "t", "vA") for t in range(NT)]
            g += [(4, j, FB, "f", "qB") for j in range(FB)] + [(5, j, FB, "f", "kB") for j in range(FB)]
            return g + [(6, t, NT, "t", "vB") for t in range(NT)]

        def d_groups(l):
            g = [(7, j, FB, "f", "qD") for j in range(FB)] + [(8, j, FB, "f", "kD") for j in range(FB)]
            return g + [(9, t, NT, "t", "vD") for t in range(NT)]

        def group_parts(name, l, groups):
            return Parts(S(name, l), ring_used, l, [(B_IN + g[0], g[1]) for g in groups],
                         {B_IN + g[0]: g[2] for g in groups})

        def merge_parts(l):
            order = [(B_MERGE + 2 * i + b, j) for i in range(2 * NBR) for j in range(FB) for b in range(2)]
            return Parts(S("merge_part", l), ring_used, l, order, FB)

        def out_parts(l):
            order = [(B_OUT + half, t) for t in range(tiles_out(l)) for half in range(2)]
            return Parts(S("out_part", l), ring_used, l, order, tiles_out(l))

        block = ctx.enter_context(nc.Block())

        class Stages:

            def __init__(self, eng):
                self.eng, self.k = eng, 0

            def leave(self):
                self.eng.drain().then_inc(stage, 1)
                self.k += 1
                self.eng.wait_ge(stage, 4 * self.k)

        state = {}

        def layer(l):
            @block.sync
            def _(sp):
                n = l * LAYER_BLOCKS

                def load(src, k=KD):
                    nonlocal n
                    if n >= RING:
                        sp.wait_ge(ring_used, n + 1 - RING)
                    sp.dma_start(ring[:, n % RING, 0:k, :], src).then_inc(ring_in[n % RING], 16)
                    n += 1

                def cols(w, c):
                    return w[:, c:c + NCH].rearrange("(k p) n -> p k n", p=P)

                for c in range(MOD_BLOCKS):
                    load(cols(A["w_mod"][l], NCH * c))
                for c in range(IN_BLOCKS):
                    load(A["w_in"][l, c])
                for half in range(2):
                    for i in range(NBR):
                        load(cols(A["w_gate"][l], i * D + half * NCH))
                        load(cols(A["w_branch"][l, i], half * NCH), FB)
                for half in range(2):
                    load(cols(A["w_out"][l], half * NCH))
                n0 = n
                with sp.Fori(0, E // 2) as i:
                    for j in range(12):
                        name = ("w_exp_gate", "w_exp_up")[j % 6 % 2] if j % 6 < 4 else "w_exp_down"
                        c = NCH * (j % 6 // 2 if j % 6 < 4 else j % 2)
                        sp.wait_ge(ring_used, i * 12 + (n0 + j + 1 - RING))
                        src = A[name][l, bass.ds(i * 2 + j // 6, 1), :, c:c + NCH]
                        sp.dma_start(ring[:, (n0 + j) % RING, :, :],
                                     src.rearrange("a (k p) n -> p (a k) n", p=P)).then_inc(ring_in[(n0 + j) % RING], 16)
                n += 6 * E
                assert n == (l + 1) * LAYER_BLOCKS

            @block.gpsimd
            def _(pool):
                st = state.setdefault("pool", Stages(pool))
                load = nc.gpsimd.dma_start

                def x_tile(l, t):
                    if l:
                        return x_d[t]
                    return A["x"][0, t * P:(t + 1) * P, :] if t < TL else A["ctx"][0, (t - TL) * P:(t - TL + 1) * P, :]

                for dst, name in ((consts[:, :], "consts"), (s2T[:, :, :], "cT"), (iotas[:, :], "iotas"))[:3 if l == 0 else 0]:
                    load(dst, A[name]).then_inc(S("const_in"), 16)
                full = tiles_out(l)
                load(mod_bias[0:2, :], A["b_mod"][l:l + 1, :].to_broadcast([2, 6 * D])).then_inc(*S("mod_bias_in", l).by(16))
                load(conv_c[:, :, :], A["conv_c"][l]).then_inc(*S("params_in", l).by(16))
                load(gate_b[:, :], A["mlstm_gate_b"][l:l + 1, :].to_broadcast([P, 4 * MH])).then_inc(*S("params_in", l).by(16))
                load(sink_b[:, :], A["attn_sink"][l:l + 1, :].to_broadcast([P, HEADS])).then_inc(*S("params_in", l).by(16))
                load(mgate_b[:, :, :], A["b_gate"][l]).then_inc(*S("params_in", l).by(16))
                pool.wait_ge(*S("mod_row", l).at(MOD_BLOCKS))
                load(mod_d[l], mod_row[0:2, :]).then_inc(*S("mod_out", l).by(16))
                pool.wait_ge(*S("mod_out", l).at(16))
                pool.wait_ge(*S("params_in", l).at(64))
                st.leave()
                for t in range(NT):
                    if t >= 2:
                        pool.wait_ge(*S("xhat", l).at(t - 1))
                    load(xin[:, t % 2, :], x_tile(l, t)).then_inc(*S(f"x_in{t % 2}", l).by(16))
                st.leave()
                nc.gpsimd.memset(cpad, 0.0).then_inc(*S("conv_zero", l).by(1))
                load(rope_t, A["rope"][:, 0:2 * LAT].rearrange("p (a n) -> p a n", a=2)).then_inc(*S("rope_in", l).by(16))
                load(rot, A["rope"][:, 2 * LAT:2 * LAT + P]).then_inc(*S("rope_in", l).by(16))
                st.leave()
                st.leave()
                pool.wait_ge(*S("rope_in", l).at(32))
                st.leave()
                def load_bias(h):
                    load(bias[:, h % 2, :], A["bias"][l, :, h, :]).then_inc(*S(f"bias_in{h % 2}", l).by(16))

                load_bias(0)
                load_bias(1)
                for u, (kind, h, n) in enumerate(units(l)):
                    lo, hi = local_keys(kind, n)
                    nk = hi - lo + CTX
                    pool.wait_ge(*S("a_rcp", l).at(u + 1))
                    nc.gpsimd.tensor_scalar(prob[:, u % 3, 0:nk], prob[:, u % 3, 0:nk], soft[:, u % 4, 6:7],
                                            None, ALU.mult).then_inc(*S("a_scaled", l).by(1))
                    if kind == "B" and n == 0 and 1 <= h < HEADS - 1:
                        pool.wait_ge(*S("a_max", l).at(u))
                        load_bias(h + 1)
                st.leave()
                for _ in range(4):
                    st.leave()
                for v, src in enumerate((mod_d[l, 0:1, 2 * D:3 * D], mod_d[l, 1:2, 2 * D:3 * D],
                                         A["ln1_g"][l:l + 1, :], A["ln1_b"][l:l + 1, :])):
                    load(rows1[:, v, :], src.to_broadcast([P, D])).then_inc(*S("rows1_in", l).by(16))
                for t in range(full):
                    load(x1[:, t, :], x_tile(l, t)).then_inc(*S("x1_in", l).by(16))
                pool.wait_ge(*S("rows1_in", l).at(64))
                pool.wait_ge(*S("x1_in", l).at(16 * full))
                st.leave()
                load(wr, A["w_router"][l].rearrange("(k p) e -> p k e", p=P)).then_inc(*S("router_in", l).by(16))
                pool.wait_ge(*S("slots", l).at(1))
                for v, row in enumerate((slotR, affR)):
                    load(slot_d[l, v, :, 0:full * P], row[0:E, 0:full * P]).then_inc(*S("slots_out", l).by(16))
                pool.wait_ge(*S("slots_out", l).at(32))
                pool.wait_ge(*S("router_in", l).at(16))
                st.leave()
                st.leave()
                for v, src in enumerate((mod_d[l, 0:1, 5 * D:6 * D], mod_d[l, 1:2, 5 * D:6 * D],
                                         A["ln2_g"][l:l + 1, :], A["ln2_b"][l:l + 1, :])):
                    load(rows2[:, v, :], src.to_broadcast([P, D])).then_inc(*S("rows2_in", l).by(16))
                nc.gpsimd.memset(acc, 0.0).then_inc(*S("acc_zero", l).by(1))
                with turns(pool, E // 2) as i:
                    for j in range(2):
                        e = i * 2 + j
                        pool.wait_ge(*S("e_put", l).at(i * 2 + j + 1))
                        for v in range(2):
                            load(pair[0:CAPL, v, 0:LAT], slot_d[l, v, bass.ds(e, 1), 0:LAT].to_broadcast([CAPL, LAT])
                                 ).then_inc(*S("pair_in", l).by(16))
                            if full == NT:
                                load(pair[CAPL:CAP, v, LAT:TOK],
                                     slot_d[l, v, bass.ds(e, 1), LAT:TOK].to_broadcast([CAPC, CTX])
                                     ).then_inc(*S("pair_in", l).by(16))
                        pool.wait_ge(ring_used, i * 12 + (l * LAYER_BLOCKS + B_EXP + 6 * j - 2))
                        for s, src in enumerate((xgA, xgB)):
                            nc.gpsimd.tensor_copy(xg[:, s * 4:s * 4 + 4, :],
                                                  src[:, :, bass.ds(e, 1), :].rearrange("p k a c -> p k (a c)")
                                                  ).then_inc(*S("xg", l).by(1))
                pool.wait_ge(*S("rows2_in", l).at(64))
                st.leave()
                for t in range(full):
                    pool.wait_ge(*S("x2", l).at(t + 1))
                    dst = x_d[t] if l < DEPTH - 1 else out[0, t * P:(t + 1) * P, :]
                    load(dst, x1[:, t, :]).then_inc(*S("x_out", l).by(16))
                pool.wait_ge(*S("x_out", l).at(16 * full))
                st.leave()

            @block.tensor
            def _(pe):
                st = state.setdefault("pe", Stages(pe))
                mm = nc.tensor.matmul
                n = l * LAYER_BLOCKS
                if l == 0:
                    pe.wait_ge(S("const_in"), 48)
                    pe.wait_ge(S("silu"), 1)

                def take():
                    nonlocal n
                    pe.wait_ge(ring_in[n % RING], 16 * (n // RING + 1))
                    n += 1
                    return (n - 1) % RING

                def feature_major(bank, slot, c, kb, src, toks):
                    for a, b, bk in toks:
                        for k in range(kb):
                            last = mm(ps[:, bank + bk, 0:b - a], ring[:, slot, k, c:c + P], src[:, k, a:b],
                                      start=k == 0, stop=k == kb - 1)
                    return last

                def token_major(dst, slot, c0, c1, src, t, kb=KD):
                    for k in range(kb):
                        last = mm(dst, src[:, k, t * P:(t + 1) * P], ring[:, slot, k, c0:c1], start=k == 0, stop=k == kb - 1)
                    return last

                full = tiles_out(l)
                even = [(0, TOK // 2, 0), (TOK // 2, TOK, 1)]
                some = even if full == NT else [(0, LAT, 0)]
                for c in range(MOD_BLOCKS):
                    s = take()
                    if c >= 2:
                        pe.wait_ge(*S("mod_row", l).at(c - 1))
                    for k in range(KD):
                        last = mm(ps[0:2, c % 2, :], s2T[:, k, :], ring[:, s, k, :], start=k == 0, stop=k == KD - 1)
                    last.then_inc(ring_used, 1)
                pe.wait_ge(*S("mod_row", l).at(MOD_BLOCKS))
                for v, part in enumerate((0, 1, 3, 4)):
                    for k in range(KD):
                        o = (v * KD + k) * 2
                        last = nc.tensor.transpose(ps[:, 2, o:o + 2], mod_row[0:2, part * D + k * P:part * D + (k + 1) * P],
                                                   ident[0:2, 0:2])
                last.then_inc(*S("mod_cols", l).by(1))
                st.leave()
                for t in range(NT):
                    pe.wait_ge(*S("xhat", l).at(t + 1))
                    if t >= 2:
                        pe.wait_ge(*S("h_done", l).at(t - 1))
                    for k in range(KD):
                        last = nc.tensor.transpose(psf[:, t % 2 * D + k * P:t % 2 * D + (k + 1) * P],
                                                   xhat[:, t % 2, k * P:(k + 1) * P], ident)
                    last.then_inc(*S("xhat_T", l).by(1))
                st.leave()
                pa = conv_parts(l)
                sa, sg = take(), take()
                toks = [(0, LAT, 0), (LAT, TOK, 1)] if full == NT else [(0, LAT, 0)]
                for j in range(FB):
                    if j >= 2:
                        pe.wait_ge(*S("conv_glu", l).at(j - 1))
                    feature_major(4 * (j % 2), sa, j * P, KD, h_v, toks).then_inc(*pa.by(B_IN, j))
                    feature_major(4 * (j % 2) + 2, sg, j * P, KD, h_v, toks).then_inc(*pa.by(B_IN + 1, j))
                st.leave()

                def project(name, groups, done):
                    pa = group_parts(name, l, groups)
                    block, s = None, None
                    for g, (b, j, _, kind, what) in enumerate(groups):
                        if b != block:
                            block, s = b, take()
                        if g >= 4:
                            pe.wait_ge(*done.at(g - 3))
                        bank = 2 * (g % 4)
                        if kind == "f":
                            last = feature_major(bank, s, j * P, KD, h_v, some if what[0] == "q" else even)
                        elif what == "vA":
                            last = token_major(ps[:, bank, 0:P + 4 * MH], s, 2 * P, 3 * P + 4 * MH, h_v, j - 2)
                        else:
                            last = token_major(ps[:, bank, :], s, 0, BW, h_v, j)
                        last.then_inc(*pa.by(B_IN + b, j))

                project("ab_part", ab_groups(l), S("ab_out", l))
                st.leave()
                for j in range(6):
                    if j >= 2:
                        pe.wait_ge(*S("rope_done", l).at(j - 1))
                    src = y_v[0][:, j, 0:LAT] if j < FB else kA[:, j - FB, 0:LAT]
                    mm(ps[:, j % 2, :], rot, src, start=True, stop=True).then_inc(*S("rope_rot", l).by(1))
                cuts = even if full == NT else [(0, LAT, 0)]
                for a, b, bk in cuts:
                    for j in range(FB):
                        last = mm(ps[:, 2 + bk, 0:b - a], ones, y_v[2][:, j, a:b], start=j == 0, stop=j == FB - 1)
                last.then_inc(*S("conv_sum", l).by(1))
                for j in range(FB):
                    pe.wait_ge(*S("conv_sq", l).at(j + 1))
                    for a, b, bk in cuts:
                        last = mm(ps[:, 4 + bk, 0:b - a], ones, csq[:, j % 2, a:b], start=j == 0, stop=j == FB - 1)
                    last.then_inc(*S("conv_sumsq", l).by(1))
                st.leave()
                us = units(l)
                for s in range(len(us) + 3):
                    if s < len(us):
                        kind, h, t = us[s]
                        hp = h % 2 * HD
                        lo, hi = local_keys(kind, t)
                        if s >= 2:
                            pe.wait_ge(*S("a_exp", l).at(s - 1))
                        q = y_v["AB".index(kind)][hp:hp + HD, h // 2, t * P:(t + 1) * P]
                        k = kA[hp:hp + HD, h // 4, :] if kind == "A" else kB[hp:hp + HD, h // 2, :]
                        if hi > lo:
                            mm(ps[:, 2 * (s % 2), 0:hi - lo], q, k[:, lo:hi], start=True, stop=True)
                        mm(ps[:, 2 * (s % 2) + 1, 0:CTX], q, k[:, LAT:TOK], start=True, stop=True).then_inc(*S("a_scores", l).by(1))
                    if 2 <= s < len(us) + 2:
                        u = s - 2
                        lo, hi = local_keys(us[u][0], us[u][2])
                        pe.wait_ge(*S("a_scaled", l).at(u + 1))
                        if u >= 1:
                            pe.wait_ge(*S("a_probT", l).at(u))
                        for b in range((hi - lo + CTX) // P):
                            last = nc.tensor.transpose(psf[:, 4 * 512 + b * P:4 * 512 + (b + 1) * P],
                                                       prob[:, u % 3, b * P:(b + 1) * P], ident)
                        last.then_inc(*S("a_turned", l).by(1))
                    if s >= 3:
                        u = s - 3
                        kind, h, t = us[u]
                        lo, hi = local_keys(kind, t)
                        tiles = list(range(lo // P, hi // P)) + list(range(TL, NT))
                        pe.wait_ge(*S("a_probT", l).at(u + 1))
                        if u >= 2:
                            pe.wait_ge(*S("a_out", l).at(u - 1))
                        for b, kt in enumerate(tiles):
                            v = vA[:, kt, h // 4 * HD:h // 4 * HD + HD] if kind == "A" else vB[:, kt, h * HD:(h + 1) * HD]
                            last = mm(ps[0:HD, 6 + u % 2, 0:P], v, probT[:, u % 2, b * P:(b + 1) * P],
                                      start=b == 0, stop=b == len(tiles) - 1)
                        last.then_inc(*S("a_values", l).by(1))
                st.leave()
                project("d_part", d_groups(l), S("d_out", l))
                st.leave()
                for d, tri in enumerate((upper, lower)):
                    mm(ps[:, 0, d * NT * MH:(d + 1) * NT * MH], tri, lf_c[:, :, d * MH:(d + 1) * MH], start=True, stop=True)
                mm(ps[:, 1, 0:NT * MU], ones, lf_c[:, :, :], start=True, stop=True).then_inc(*S("m_cum", l).by(1))
                fwd, bwd = [4, 5, 0, 1, 2, 3], [5, 4, 3, 2, 1, 0]
                for j in range(NT):
                    chunk = (fwd[j], bwd[j])
                    outs = fwd[j] < full
                    for half in range(2):
                        pe.wait_ge(*S("m_diag", l).at(2 * j + half + 1))
                        for g in range(2):
                            last = mm(ps[:, g, :], ones, mA[:, 4 * g:4 * g + 4, :], start=True, stop=True)
                        last.then_inc(*S("m_rows", l).by(1))
                    if outs:
                        for u in range(MU):
                            c = slice(chunk[u // MH] * P, (chunk[u // MH] + 1) * P)
                            last = mm(psf[:, 2 * 512 + u * P:2 * 512 + (u + 1) * P], kD[:, u % MH, c], y_v[3][:, u % MH, c],
                                      start=True, stop=True)
                        last.then_inc(*S("m_scores", l).by(1))
                    pe.wait_ge(*S("m_arg", l).at(j + 1))
                    for u in range(MU):
                        c = slice(chunk[u // MH] * P, (chunk[u // MH] + 1) * P)
                        last = nc.tensor.transpose(psf[:, u * P:(u + 1) * P], kD[:, u % MH, c], ident)
                    last.then_inc(*S("m_keys", l).by(1))
                    if outs:
                        pe.wait_ge(*S("m_weights", l).at(count_outs(l, fwd, j) + 1))
                        for d in range(2):
                            if d == 1:
                                pe.wait_ge(*S("m_num", l).at(2 * count_outs(l, fwd, j) + 1))
                            for q in range(MH):
                                u, o = d * MH + q, q % 2 * MV
                                mm(ps[:, 4 + q // 2, o:o + MV], mB[:, u, :], vD[:, chunk[d], q, :], start=True, stop=True)
                                last = mm(ps[:, 6 + q // 2, o:o + MV], y_v[3][:, q, chunk[d] * P:(chunk[d] + 1) * P],
                                          cst[:, u, :], start=True, stop=True)
                            last.then_inc(*S("m_mm", l).by(1))
                    pe.wait_ge(*S("m_kw", l).at(j + 1))
                    for d in range(2):
                        if d == 1:
                            pe.wait_ge(*S("m_state", l).at(2 * j + 1))
                        for q in range(MH):
                            o = q % 2 * MV
                            last = mm(ps[:, 2 + q // 2, o:o + MV], mA[:, d * MH + q, :], vD[:, chunk[d], q, :],
                                      start=True, stop=True)
                        last.then_inc(*S("m_outer", l).by(1))
                    pe.wait_ge(*S("m_state", l).at(2 * j + 2))
                st.leave()
                s = take()
                for t in range(full + 1):
                    if t < full:
                        if t >= 2:
                            pe.wait_ge(*S("o_sig", l).at(t - 1))
                        last = token_major(ps[:, t % 2, :], s, 0, BW, h_v, t)
                        last.then_inc(*(S("o_mm", l).by(1) if t < full - 1 else (ring_used, 1)))
                    if t:
                        pe.wait_ge(*S("o_gated", l).at(t))
                        if t >= 3:
                            pe.wait_ge(*S("o_out", l).at(t - 2))
                        for b in range(FB):
                            last = nc.tensor.transpose(ps[:, 2 + (t - 1) % 2, b * P:(b + 1) * P],
                                                       hD[:, t - 1, b * P:(b + 1) * P], ident)
                        last.then_inc(*S("o_turned", l).by(1))
                st.leave()
                pa = merge_parts(l)
                g = 0
                for half in range(2):
                    for i in range(NBR):
                        b = B_MERGE + 2 * (half * NBR + i)
                        sg, sbr = take(), take()
                        for j in range(FB):
                            if g >= 2:
                                pe.wait_ge(*S("z_part", l).at(g - 1))
                            feature_major(4 * (g % 2), sg, j * P, KD, h_v, some).then_inc(*pa.by(b, j))
                            feature_major(4 * (g % 2) + 2, sbr, j * P, FB, y_v[i], some).then_inc(*pa.by(b + 1, j))
                            g += 1
                st.leave()
                op = out_parts(l)
                slots = take(), take()
                for t in range(full + 1):
                    if t < full:
                        if t >= 2:
                            pe.wait_ge(*S("p_y", l).at(t - 1))
                        for half in range(2):
                            token_major(ps[:, 2 * (t % 2) + half, :], slots[half], 0, NCH, zT, t
                                        ).then_inc(*op.by(B_OUT + half, t))
                    if t:
                        pe.wait_ge(*S("xn", l).at(t))
                        if t >= 3:
                            pe.wait_ge(*S("h2_done", l).at(t - 2))
                        for k in range(KD):
                            o = 2 * D + (t - 1) % 2 * D + k * P
                            last = nc.tensor.transpose(psf[:, o:o + P], xn[:, (t - 1) * D + k * P:(t - 1) * D + (k + 1) * P], ident)
                        last.then_inc(*S("xn_T", l).by(1))
                st.leave()
                pe.wait_ge(*S("router_in", l).at(16))
                for t in range(full):
                    for k in range(KD):
                        last = mm(ps[:, 0, t * E:(t + 1) * E], h_v[:, k, t * P:(t + 1) * P], wr[:, k, :],
                                  start=k == 0, stop=k == KD - 1)
                last.then_inc(*S("r_logits", l).by(1))
                pe.wait_ge(*S("r_aff", l).at(1))
                for t in range(full):
                    last = nc.tensor.transpose(psf[0:E, 2 * 512 + t * P:2 * 512 + (t + 1) * P], aff[:, t, :], ident)
                last.then_inc(*S("r_affT", l).by(1))
                pe.wait_ge(*S("slots", l).at(1))
                for t in range(full):
                    last = nc.tensor.transpose(ps[:, 4, t * E:(t + 1) * E], slotR[0:E, t * P:(t + 1) * P], ident[0:E, 0:E])
                last.then_inc(*S("r_slotT", l).by(1))
                st.leave()
                g = 0
                for k in range(KD):
                    for part in range(3 if full == NT else 2):
                        if g >= 4:
                            pe.wait_ge(*S("g_out", l).at(g - 3))
                        ts = range(TL) if part < 2 else range(TC)
                        for t in ts:
                            tok = (t if part < 2 else TL + t) * D + k * P
                            rhs = pick_l[:, t, 8 * part:8 * part + 8, :] if part < 2 else pick_c[:, t, :, :]
                            last = mm(ps[:, g % 4, :], xn[:, tok:tok + P], rhs, start=t == 0, stop=t == ts[-1])
                        last.then_inc(*S("g_mm", l).by(1))
                        g += 1
                st.leave()
                m = CAP if full == NT else CAPL
                ncomb = 2 * full
                n0 = n
                pe.drain().then_inc(*S("e_comb", l).by(1))
                with turns(pe, E // 2) as i:
                    for j in range(2):
                        def ready(b):
                            q = n0 + 6 * j + b
                            pe.wait_ge(ring_in[q % RING], i * (16 * 12 // RING) + 16 * (q // RING + 1))
                            return q % RING

                        pe.wait_ge(*S("xg", l).at(i * 4 + 2 * j + 2))
                        pe.wait_ge(*S("e_acc", l).at(i * 2 * ncomb + ncomb * j + 1))
                        for b in range(4):
                            s = ready(b)
                            for k in range(KD):
                                last = mm(ps[0:m, b, :], xg[:, k, 0:m], ring[:, s, k, :], start=k == 0, stop=k == KD - 1)
                            last.then_inc(ring_used, 1)
                        for half in range(2):
                            pe.wait_ge(*S("e_hid", l).at(i * 4 + 2 * j + half + 1))
                            for b in range(4):
                                k = 4 * half + b
                                dst, src = ps[:, 4 + 3 * half, b * CAP:b * CAP + m], hid[0:m, k * P:(k + 1) * P]
                                if b == 0:
                                    mm(dst, src, ident[0:m, 0:m], start=True, stop=True)
                                else:
                                    last = nc.tensor.transpose(dst, src, ident[0:m, 0:m])
                            last.then_inc(*S("e_turned", l).by(1))
                        pe.wait_ge(*S("e_hidT", l).at(i * 4 + 2 * j + 2))
                        for b in range(2):
                            s = ready(4 + b)
                            for k in range(KD):
                                last = mm(ps[0:m, 5 + b, :], hidT[:, k, 0:m], ring[:, s, k, :], start=k == 0, stop=k == KD - 1)
                            last.then_inc(ring_used, 1)
                        pe.wait_ge(*S("e_put", l).at(i * 2 + j + 2))
                        for b in range(2):
                            pe.wait_ge(*S("e_y", l).at(i * 4 + 2 * j + b + 1))
                            for t in range(full):
                                c = b * full + t
                                if c >= 4:
                                    pe.wait_ge(*S("e_acc", l).at(i * 2 * ncomb + (ncomb * j + c - 2)))
                                r = slice(0, CAPL) if t < TL else slice(CAPL, CAP)
                                mm(ps[:, c % 4, :], put[r, t * P:(t + 1) * P], ysb[r, b * NCH:(b + 1) * NCH],
                                   start=True, stop=True).then_inc(*S("e_comb", l).by(1))
                n += 6 * E
                st.leave()
                st.leave()

            @block.scalar
            def _(act):
                st = state.setdefault("act", Stages(act))
                fn = nc.scalar.activation
                own = state.setdefault("act_own", Chain(act, S("act_own")))
                if l == 0:
                    act.wait_ge(S("const_in"), 48)
                    fn(s2T[:, :, :], s2T[:, :, :], ACT.Silu).then_inc(S("silu"), 1)
                full = tiles_out(l)
                ctx_out = full == NT

                def even(v):
                    return v.rearrange("p (a n) -> p a n", a=2)

                st.leave()
                def modulate(t, base, v, done):
                    s = 0 if t < TL else 1
                    for k in range(KD):
                        last = fn(h_v[:, k, t * P:(t + 1) * P], psf[:, base + k * P:base + (k + 1) * P], ACT.Identity,
                                  bias=modc[:, v, k, s:s + 1], scale=modc[:, v + 1, k, s:s + 1])
                    last.then_inc(*done.by(1))

                for t in range(NT + 1):
                    if t < NT:
                        act.wait_ge(*S("var", l).at(t + 1))
                        fn(stat[:, t % 2, 15:16], stat[:, t % 2, 14:15], ACT.Sqrt).then_inc(*S("std", l).by(1))
                    if t:
                        act.wait_ge(*S("xhat_T", l).at(t))
                        modulate(t - 1, (t - 1) % 2 * D, 0, S("h_done", l))
                st.leave()
                pa = conv_parts(l)
                for j in range(FB):
                    act.wait_ge(*pa.of(B_IN + 1, j))
                    if j >= 1:
                        act.wait_ge(*S("conv_glu", l).at(j))
                    b = 4 * (j % 2) + 2
                    last = fn(csg[:, 0:LAT], ps[:, b, :], ACT.Sigmoid)
                    if ctx_out:
                        last = fn(csg[:, LAT:TOK], ps[:, b + 1, 0:CTX], ACT.Sigmoid)
                    last.then_inc(*S("conv_sig", l).by(1))
                st.leave()

                def copies(name, groups, done):
                    pa = group_parts(name, l, groups)
                    for g, (b, j, _, kind, what) in enumerate(groups):
                        act.wait_ge(*pa.of(B_IN + b, j))
                        bank = 2 * (g % 4)
                        if kind == "f":
                            dst = {"qA": y_v[0], "kA": kA, "qB": y_v[1], "kB": kB, "qD": y_v[3], "kD": kD}[what]
                            scale = QSCALE if what in ("qA", "qB") else MSCALE if what == "kD" else 1.0
                            if what[0] == "q" and not ctx_out:
                                last = fn(dst[:, j, 0:LAT], ps[:, bank, :], ACT.Copy, scale=scale)
                            else:
                                last = fn(even(dst[:, j, :]), ps[:, bank:bank + 2, 0:TOK // 2], ACT.Copy, scale=scale)
                        elif what == "vA":
                            fn(vA[:, j - 2, :], ps[:, bank, 0:P], ACT.Copy)
                            last = fn(gates[:, j - 2, :], ps[:, bank, P:P + 4 * MH], ACT.Copy)
                        elif what == "vB":
                            last = fn(vB[:, j, :], ps[:, bank, :], ACT.Copy)
                        else:
                            last = fn(vD[:, j, :, 0:P], ps[:, bank, :].rearrange("p (h n) -> p h n", h=MH), ACT.Copy)
                        last.then_inc(*done.by(1))

                copies("ab_part", ab_groups(l), S("ab_out", l))
                st.leave()
                nt = TOK if ctx_out else LAT
                for j in range(FB):
                    act.wait_ge(*S("conv_cent", l).at(j + 1))
                    if j >= 2:
                        act.wait_ge(*S("conv_sumsq", l).at(j - 1))
                    fn(csq[:, j % 2, 0:nt], y_v[2][:, j, 0:nt], ACT.Square).then_inc(*S("conv_sq", l).by(1))
                act.wait_ge(*S("conv_var", l).at(1))
                fn(cstd[:, 0:nt], cstd[:, 0:nt], ACT.Sqrt).then_inc(*S("conv_std", l).by(1))
                for j in range(FB):
                    act.wait_ge(*S("conv_normed", l).at(j + 1))
                    fn(y_v[2][:, j, 0:nt], y_v[2][:, j, 0:nt], ACT.Silu, bias=conv_c[:, j, KS + 2:KS + 3],
                       scale=conv_c[:, j, KS + 1:KS + 2])
                st.leave()
                us = units(l)
                for s in range(len(us) + 2):
                    if s < len(us):
                        kind, h, t = us[s]
                        lo, hi = local_keys(kind, t)
                        nl = hi - lo
                        sf = soft[:, s % 4, :]
                        act.wait_ge(*S("a_max", l).at(s + 1))
                        if nl:
                            fn(prob[:, s % 3, 0:nl], prob[:, s % 3, 0:nl], ACT.Exp, bias=sf[:, 2:3], accum_out=sf[:, 3:4])
                        if kind == "A":
                            fn(sf[:, 5:6], sink_b[:, h:h + 1], ACT.Exp, bias=sf[:, 2:3])
                        fn(prob[:, s % 3, nl:nl + CTX], ps[:, 2 * (s % 2) + 1, 0:CTX], ACT.Exp, bias=sf[:, 2:3],
                           accum_out=sf[:, 4:5]).then_inc(*S("a_exp", l).by(1))
                    if s >= 2:
                        u = s - 2
                        lo, hi = local_keys(us[u][0], us[u][2])
                        act.wait_ge(*S("a_turned", l).at(u + 1))
                        if u >= 2:
                            act.wait_ge(*S("a_values", l).at(u - 1))
                        fn(probT[:, u % 2, 0:hi - lo + CTX], psf[:, 4 * 512:4 * 512 + hi - lo + CTX], ACT.Copy
                           ).then_inc(*S("a_probT", l).by(1))
                st.leave()
                act.wait_ge(*S("m_abs", l).at(1))
                own(fn(lt_c[:, :, :], lt_c[:, :, :], ACT.Exp, scale=-1.0))
                own.wait()
                fn(lt_c[:, :, :], lt_c[:, :, :], ACT.Ln, bias=1.0).then_inc(*S("m_log", l).by(1))
                copies("d_part", d_groups(l), S("d_out", l))
                st.leave()
                fwd = [4, 5, 0, 1, 2, 3]
                for j in range(NT):
                    outs = fwd[j] < full
                    act.wait_ge(*S("m_diag", l).at(2 * j + 2))
                    fn(ex_c[:, :, :], ex_in[:, :, :], ACT.Exp).then_inc(*S("m_exps", l).by(1))
                    if outs:
                        act.wait_ge(*S("m_arg2", l).at(count_outs(l, fwd, j) + 1))
                        fn(mB[:, :, :], mB[:, :, :], ACT.Exp).then_inc(*S("m_gate", l).by(1))
                    act.wait_ge(*S("m_exps", l).at(j + 1))
                    act.wait_ge(*S("m_keys", l).at(j + 1))
                    for u in range(MU):
                        last = fn(mA[:, u, :], psf[:, u * P:(u + 1) * P], ACT.Copy, scale=ex_c[:, 2, u:u + 1])
                    last.then_inc(*S("m_kw", l).by(1))
                    if outs:
                        for d in range(2):
                            c = 2 * count_outs(l, fwd, j) + d
                            act.wait_ge(*S("m_mm", l).at(c + 1))
                            for q in range(MH):
                                u, o = d * MH + q, q % 2 * MV
                                last = fn(mC[:, u, :], ps[:, 6 + q // 2, o:o + MV], ACT.Copy, scale=ex_c[:, 0, u:u + 1])
                            last.then_inc(*S("m_carried", l).by(1))
                st.leave()
                for t in range(full):
                    if t < full - 1:
                        act.wait_ge(*S("o_mm", l).at(t + 1))
                    else:
                        act.wait_ge(ring_used, l * LAYER_BLOCKS + B_IN + IN_BLOCKS)
                    if t >= 2:
                        act.wait_ge(*S("o_gated", l).at(t - 1))
                    fn(sig_o[:, t % 2, :], ps[:, t % 2, :], ACT.Sigmoid).then_inc(*S("o_sig", l).by(1))
                st.leave()
                pa = merge_parts(l)
                g = 0
                for half in range(2):
                    for i in range(NBR):
                        for j in range(FB):
                            act.wait_ge(*pa.of(B_MERGE + 2 * (half * NBR + i), j))
                            if g >= 2:
                                act.wait_ge(*S("z_part", l).at(g - 1))
                            bank, bcol = 4 * (g % 2), mgate_b[:, i, half * FB + j:half * FB + j + 1]
                            if ctx_out:
                                last = fn(even(mg_s[:, g % 2, :]), ps[:, bank:bank + 2, 0:TOK // 2], ACT.Sigmoid, bias=bcol)
                            else:
                                last = fn(mg_s[:, g % 2, 0:LAT], ps[:, bank, :], ACT.Sigmoid, bias=bcol)
                            last.then_inc(*S("z_gate", l).by(1))
                            g += 1
                st.leave()
                for t in range(full + 1):
                    if t < full:
                        for v in range(2):
                            act.wait_ge(*S("p_var", l).at(2 * t + v + 1))
                            fn(stat[:, v, 15:16], stat[:, v, 14:15], ACT.Sqrt).then_inc(*S("p_std", l).by(1))
                    if t:
                        act.wait_ge(*S("xn_T", l).at(t))
                        modulate(t - 1, 2 * D + (t - 1) % 2 * D, 2, S("h2_done", l))
                st.leave()
                act.wait_ge(*S("r_cent", l).at(1))
                fn(aff[:, 0:full, :], aff[:, 0:full, :], ACT.Exp).then_inc(*S("r_exp", l).by(1))
                st.leave()
                g = 0
                for k in range(KD):
                    for part in range(3 if ctx_out else 2):
                        act.wait_ge(*S("g_mm", l).at(g + 1))
                        s = part // 2
                        dst = (xgA if k < 4 else xgB)[:, k % 4, :, :]
                        dst = dst[:, 8 * part:8 * part + 8, 0:CAPL] if part < 2 else dst[:, :, CAPL:CAP]
                        fn(dst, ps[:, g % 4, :].rearrange("p (e c) -> p e c", e=E if s else 8), ACT.Identity,
                           bias=modc[:, 2, k, s:s + 1], scale=modc[:, 3, k, s:s + 1]).then_inc(*S("g_out", l).by(1))
                        g += 1
                st.leave()
                m = CAP if ctx_out else CAPL
                r0 = l * LAYER_BLOCKS + B_EXP
                with turns(act, E // 2) as i:
                    for j in range(2):
                        for half in range(2):
                            act.wait_ge(ring_used, i * 12 + (r0 + 6 * j + 2 * half + 1))
                            fn(hid[0:m, half * NCH:(half + 1) * NCH], ps[0:m, 2 * half, :], ACT.Silu).then_inc(*S("e_sil", l).by(1))
                        for half in range(2):
                            act.wait_ge(*S("e_turned", l).at(i * 4 + 2 * j + half + 1))
                            fn(hidT[:, 4 * half:4 * half + 4, 0:m],
                               ps[:, 4 + 3 * half, 0:4 * CAP].rearrange("p (k c) -> p k c", k=4)[:, :, 0:m],
                               ACT.Copy).then_inc(*S("e_hidT", l).by(1))
                        for half in range(2):
                            act.wait_ge(ring_used, i * 12 + (r0 + 6 * j + 4 + half + 1))
                            act.wait_ge(*S("e_comb", l).at(i * 4 * full + 2 * full * j + 1))
                            fn(ysb[0:m, half * NCH:(half + 1) * NCH], ps[0:m, 5 + half, :], ACT.Copy).then_inc(*S("e_y", l).by(1))
                st.leave()
                for t in range(full):
                    act.wait_ge(*S("q_var", l).at(t + 1))
                    fn(stat[:, 0, 15:16], stat[:, 0, 14:15], ACT.Sqrt).then_inc(*S("q_std", l).by(1))
                st.leave()

            @block.vector
            def _(dve):
                st = state.setdefault("dve", Stages(dve))
                V = nc.vector
                own = state.setdefault("dve_own", Chain(dve, S("dve_own")))

                full = tiles_out(l)
                ctx_out = full == NT
                nt = full * P
                r0 = l * LAYER_BLOCKS

                def even(v):
                    return v.rearrange("p (a n) -> p a n", a=2)

                def result(bank, v):
                    if ctx_out:
                        return ps[:, bank:bank + 2, 0:TOK // 2], even(v)
                    return ps[:, bank, :], v[:, 0:LAT]

                def standardise(src, dst, sf, var, std, count):
                    for half in range(2):
                        own(V.bn_stats(sf[:, 6 * half:6 * half + 6], src[:, half * 512:(half + 1) * 512]))
                    own.wait()
                    own(V.bn_aggr(sf[:, 12:14], sf[:, 0:12]))
                    own.wait()
                    V.tensor_scalar(sf[:, 14:15], sf[:, 13:14], EPS, None, ALU.add).then_inc(*var.by(1))
                    dve.wait_ge(*std.at(count))
                    own(V.reciprocal(sf[:, 16:17], sf[:, 15:16]))
                    own.wait()
                    return V.tensor_scalar(dst, src, sf[:, 12:13], sf[:, 16:17], ALU.subtract, ALU.mult)

                dve.wait_ge(*S("mod_bias_in", l).at(16))
                for c in range(MOD_BLOCKS):
                    dve.wait_ge(ring_used, r0 + c + 1)
                    V.tensor_tensor(mod_row[0:2, c * NCH:(c + 1) * NCH], ps[0:2, c % 2, :],
                                    mod_bias[0:2, c * NCH:(c + 1) * NCH], ALU.add).then_inc(*S("mod_row", l).by(1))
                dve.wait_ge(*S("mod_cols", l).at(1))
                for v in range(4):
                    src = ps[:, 2, v * 2 * KD:(v + 1) * 2 * KD].rearrange("p (k s) -> p k s", k=KD)
                    V.tensor_scalar(modc[:, v, :, :], src, float(v % 2), None, ALU.add)
                st.leave()
                for t in range(NT):
                    dve.wait_ge(*S(f"x_in{t % 2}", l).at(16 * (t // 2 + 1)))
                    if t >= 2:
                        dve.wait_ge(*S("xhat_T", l).at(t - 1))
                    standardise(xin[:, t % 2, :], xhat[:, t % 2, :], stat[:, t % 2, :], S("var", l), S("std", l), t + 1
                                ).then_inc(*S("xhat", l).by(1))
                st.leave()
                dve.wait_ge(*S("conv_zero", l).at(1))
                for j in range(FB):
                    dve.wait_ge(*S("conv_sig", l).at(j + 1))
                    b = 4 * (j % 2)
                    last = V.tensor_tensor(cpad[:, j, HALO:HALO + LAT], ps[:, b, :], csg[:, 0:LAT], ALU.mult)
                    if ctx_out:
                        last = V.tensor_tensor(cpad[:, j, LSEG + HALO:LSEG + HALO + CTX], ps[:, b + 1, 0:CTX],
                                               csg[:, LAT:TOK], ALU.mult)
                    last.then_inc(*S("conv_glu", l).by(1))
                st.leave()
                segs = [(0, 0, LAT), (LSEG, LAT, CTX)] if ctx_out else [(0, 0, LAT)]
                for tap in range(KS):
                    for j in range(FB):
                        for src, dst, size in segs:
                            y = y_v[2][:, j, dst:dst + size]
                            x = cpad[:, j, src + tap:src + tap + size]
                            if tap == 0:
                                own(V.tensor_scalar(y, x, conv_c[:, j, 0:1], conv_c[:, j, KS:KS + 1], ALU.mult, ALU.add))
                            else:
                                own.wait(FB * len(segs) - 1)
                                own(V.scalar_tensor_tensor(y, x, conv_c[:, j, tap:tap + 1], y, ALU.mult, ALU.add))
                st.leave()
                dve.wait_ge(*S("rope_in", l).at(32))
                for j in range(6):
                    q = y_v[0][:, j, 0:LAT] if j < FB else kA[:, j - FB, 0:LAT]
                    dve.wait_ge(*S("rope_rot", l).at(j + 1))
                    V.tensor_tensor(rope_s[:, j % 2, :], ps[:, j % 2, :], rope_t[:, 1, :], ALU.mult).then_inc(*S("rope_done", l).by(1))
                    own(V.tensor_tensor(q, q, rope_t[:, 0, :], ALU.mult))
                    own.wait()
                    dve.wait_ge(*S("rope_done", l).at(j + 1))
                    V.tensor_tensor(q, q, rope_s[:, j % 2, :], ALU.add)
                dve.wait_ge(*S("conv_sum", l).at(1))
                for j in range(FB):
                    p_, y = result(2, y_v[2][:, j, :])
                    V.scalar_tensor_tensor(y, p_, -1.0 / BW, y, ALU.mult, ALU.add).then_inc(*S("conv_cent", l).by(1))
                dve.wait_ge(*S("conv_sumsq", l).at(FB))
                p_, y = result(4, cstd)
                V.tensor_scalar(y, p_, 1.0 / BW, EPS, ALU.mult, ALU.add).then_inc(*S("conv_var", l).by(1))
                dve.wait_ge(*S("conv_std", l).at(1))
                own(V.reciprocal(cstd[:, 0:nt], cstd[:, 0:nt]))
                own.wait()
                dve.wait_ge(*S("conv_cent", l).at(FB))
                for j in range(FB):
                    V.tensor_tensor(y_v[2][:, j, 0:nt], y_v[2][:, j, 0:nt], cstd[:, 0:nt], ALU.mult
                                    ).then_inc(*S("conv_normed", l).by(1))
                st.leave()
                us = units(l)
                for s in range(len(us) + 3):
                    if s < len(us):
                        kind, h, t = us[s]
                        lo, hi = local_keys(kind, t)
                        nl = hi - lo
                        sf, b = soft[:, s % 4, :], 2 * (s % 2)
                        dve.wait_ge(*S("a_scores", l).at(s + 1))
                        if s >= 3:
                            dve.wait_ge(*S("a_turned", l).at(s - 2))
                        if kind == "B" and t == 0:
                            dve.wait_ge(*S(f"bias_in{h % 2}", l).at(16 * (h // 2 + 1)))
                        if nl and kind == "A":
                            o = P if t == 0 else 0
                            own(V.tensor_tensor(prob[:, s % 3, 0:nl], ps[:, b, 0:nl], band[:, o:o + nl], ALU.add))
                        elif nl:
                            o = (LAT // GRID_W - 1 - 2 * t) * GRID_W
                            own(V.tensor_tensor(prob[:, s % 3, 0:nl], ps[:, b, 0:nl], bias[:, h % 2, o:o + nl], ALU.add))
                        own(V.tensor_reduce(sf[:, 1:2], ps[:, b + 1, 0:CTX], AX, ALU.max))
                        if nl:
                            own.wait(1)
                            own(V.tensor_reduce(sf[:, 0:1], prob[:, s % 3, 0:nl], AX, ALU.max))
                        own.wait()
                        first = sf[:, 0:1] if nl else sf[:, 1:2]
                        second = sink_b[:, h:h + 1] if kind == "A" else first
                        own(V.tensor_scalar(sf[:, 7:8], sf[:, 1:2], first, second, ALU.max, ALU.max))
                        own.wait()
                        V.tensor_scalar(sf[:, 2:3], sf[:, 7:8], -1.0, None, ALU.mult).then_inc(*S("a_max", l).by(1))
                    if 1 <= s <= len(us):
                        u = s - 1
                        kind, h, t = us[u]
                        lo, hi = local_keys(kind, t)
                        sf = soft[:, u % 4, :]
                        dve.wait_ge(*S("a_exp", l).at(u + 1))
                        total = sf[:, 4:5]
                        if hi > lo and kind == "A":
                            own(V.tensor_scalar(sf[:, 7:8], total, sf[:, 3:4], sf[:, 5:6], ALU.add, ALU.add))
                        elif hi > lo or kind == "A":
                            own(V.tensor_scalar(sf[:, 7:8], total, sf[:, 3:4] if hi > lo else sf[:, 5:6], None, ALU.add))
                        if hi > lo or kind == "A":
                            own.wait()
                            total = sf[:, 7:8]
                        V.reciprocal(sf[:, 6:7], total).then_inc(*S("a_rcp", l).by(1))
                    if s >= 3:
                        u = s - 3
                        kind, h, t = us[u]
                        hp = h % 2 * HD
                        dve.wait_ge(*S("a_values", l).at(u + 1))
                        V.tensor_copy(y_v["AB".index(kind)][hp:hp + HD, h // 2, t * P:(t + 1) * P], ps[0:HD, 6 + u % 2, 0:P]
                                      ).then_inc(*S("a_out", l).by(1))
                st.leave()
                for d in range(2):
                    c = slice(d * MH, (d + 1) * MH)
                    for x, o in ((ig_c, 8 * d), (lf_c, 8 * d + 4)):
                        own(V.tensor_tensor(x[:, :, c], gates[:, :, o:o + MH],
                                            gate_b[:, o:o + MH].unsqueeze(1).to_broadcast([P, NT, MH]), ALU.add))
                own(V.memset(vD[:, :, :, P:MV], 1.0))
                own.wait()
                V.scalar_tensor_tensor(lt_c[:, :, :], lf_c[:, :, :], -1.0, lf_c[:, :, :], ALU.mult, ALU.max
                                       ).then_inc(*S("m_abs", l).by(1))
                dve.wait_ge(*S("m_log", l).at(1))
                V.scalar_tensor_tensor(lf_c[:, :, :], lf_c[:, :, :], 0.0, lt_c[:, :, :], ALU.min, ALU.subtract)
                st.leave()
                fwd, bwd = [4, 5, 0, 1, 2, 3], [5, 4, 3, 2, 1, 0]
                own(V.memset(cst, 0.0))
                own(V.memset(m_c, 0.0))
                own(V.memset(hD, 0.0))
                dve.wait_ge(*S("m_cum", l).at(1))
                for d in range(2):
                    c = slice(d * MH, (d + 1) * MH)
                    F = ps[:, 0, d * NT * MH:(d + 1) * NT * MH].rearrange("p (t m) -> p t m", t=NT)
                    own(V.tensor_tensor(u_c[:, :, c], ig_c[:, :, c], F, ALU.subtract))
                    own(V.tensor_copy(F_c[:, :, c], F))
                own(V.tensor_copy(FL_c[:, :, :], ps[:, 1, 0:NT * MU].rearrange("p (t m) -> p t m", t=NT)))
                own.wait()
                idb = ident.unsqueeze(1).to_broadcast([P, MH, P])
                for j in range(NT):
                    chunk = (fwd[j], bwd[j])
                    outs = fwd[j] < full
                    io = count_outs(l, fwd, j)
                    dirs = [(d, slice(d * MH, (d + 1) * MH)) for d in range(2)]

                    def diagonal(col):
                        own(V.tensor_tensor(mA[:, 0:MH, :], idb, col(0).unsqueeze(2).to_broadcast([P, MH, P]), ALU.mult))
                        V.tensor_tensor(mA[:, MH:MU, :], idb, col(1).unsqueeze(2).to_broadcast([P, MH, P]), ALU.mult
                                        ).then_inc(*S("m_diag", l).by(1))

                    diagonal(lambda d: u_c[:, chunk[d], dirs[d][1]])
                    dve.wait_ge(*S("m_rows", l).at(2 * j + 1))
                    rows = ps[:, 0:2, :].rearrange("p b (q n) -> p (b q) n", q=MH)
                    own(V.tensor_reduce(cm_c[:, 1, :], rows, AX, ALU.max))
                    for d, c in dirs:
                        mask = (neg_le, neg_ge)[d]
                        own(V.tensor_tensor(mB[:, c, :], rows[:, c, :], mask.unsqueeze(1).to_broadcast([P, MH, P]), ALU.add))
                    own.wait()
                    own(V.tensor_reduce(cm_c[:, 0, :], mB, AX, ALU.max))
                    own.wait()
                    for v in range(2):
                        own(V.tensor_tensor(M_c[:, v, :], cm_c[:, v, :], m_c, ALU.max))
                    own.wait()
                    own(V.tensor_scalar(nM_c, M_c[:, 0, :], -1.0, None, ALU.mult))
                    for v in range(2):
                        own(V.tensor_tensor(ex_in[:, v, :], m_c, M_c[:, v, :], ALU.subtract))
                    for d, c in dirs:
                        own(V.tensor_tensor(ex_in[:, 2, c], u_c[:, chunk[d], c], M_c[:, 1, c], ALU.subtract))
                    own.wait()
                    for d, c in dirs:
                        own(V.tensor_tensor(ex_in[:, 3, c], nM_c[:, c], F_c[:, chunk[d], c], ALU.subtract))
                        own(V.tensor_tensor(m_c[:, c], M_c[:, 1, c], FL_c[:, chunk[d], c], ALU.add))
                    own.wait()
                    diagonal(lambda d: nM_c[:, dirs[d][1]])
                    dve.wait_ge(*S("m_rows", l).at(2 * j + 2))
                    for d, c in dirs:
                        mask = (neg_ge, neg_le)[d]
                        ins = V.tensor_tensor(mB[:, c, :], rows[:, c, :], mask.unsqueeze(1).to_broadcast([P, MH, P]), ALU.add)
                        if d:
                            ins.then_inc(*S("m_arg", l).by(1))
                        else:
                            own(ins)
                    if outs:
                        own.wait()
                        dve.wait_ge(*S("m_arg", l).at(j + 1))
                        for d, c in dirs:
                            ins = V.tensor_tensor(mB[:, c, :], mB[:, c, :],
                                                  u_c[:, chunk[d], c].unsqueeze(2).to_broadcast([P, MH, P]), ALU.add)
                            if d:
                                ins.then_inc(*S("m_arg2", l).by(1))
                            else:
                                own(ins)
                        dve.wait_ge(*S("m_gate", l).at(io + 1))
                        dve.wait_ge(*S("m_scores", l).at(io + 1))
                        V.tensor_tensor(mB, mB, ps[:, 2:4, :].rearrange("p b (q n) -> p (b q) n", q=MH), ALU.mult
                                        ).then_inc(*S("m_weights", l).by(1))
                        dve.wait_ge(*S("m_exps", l).at(j + 1))
                        for d, c in dirs:
                            dve.wait_ge(*S("m_carried", l).at(2 * io + d + 1))
                            num = mC[:, c, :].rearrange("p (a b) n -> p a (b n)", a=2)
                            V.tensor_tensor(num, num, ps[:, 4:6, 0:2 * MV], ALU.add).then_inc(*S("m_num", l).by(1))
                            dve.wait_ge(*S("m_num", l).at(2 * io + d + 1))
                            dn = mC[:, c, P:MV].rearrange("p h n -> p (h n)")
                            own(V.scalar_tensor_tensor(den[:, 0, c], dn, -1.0, dn, ALU.mult, ALU.max))
                            own.wait()
                            own(V.tensor_tensor(den[:, 1, c], den[:, 0, c], ex_c[:, 3, c], ALU.max))
                            own.wait()
                            own(V.reciprocal(den[:, 2, c], den[:, 1, c]))
                            own.wait()
                            for q in range(MH):
                                hs = hD[:, chunk[d], q * P:(q + 1) * P]
                                own(V.scalar_tensor_tensor(hs, mC[:, d * MH + q, 0:P], den[:, 2, d * MH + q:d * MH + q + 1], hs,
                                                           ALU.mult, ALU.add))
                    dve.wait_ge(*S("m_exps", l).at(j + 1))
                    for d, c in dirs:
                        dve.wait_ge(*S("m_outer", l).at(2 * j + d + 1))
                        for q in range(MH):
                            u, o = d * MH + q, q % 2 * MV
                            last = V.scalar_tensor_tensor(cst[:, u, :], cst[:, u, :], ex_c[:, 1, u:u + 1],
                                                          ps[:, 2 + q // 2, o:o + MV], ALU.mult, ALU.add)
                            if q < MH - 1:
                                own(last)
                        last.then_inc(*S("m_state", l).by(1))
                    own.wait()
                    dve.wait_ge(*S("m_state", l).at(2 * j + 2))
                st.leave()
                for t in range(full):
                    dve.wait_ge(*S("o_sig", l).at(t + 1))
                    V.tensor_tensor(hD[:, t, :], hD[:, t, :], sig_o[:, t % 2, :], ALU.mult).then_inc(*S("o_gated", l).by(1))
                    dve.wait_ge(*S("o_turned", l).at(t + 1))
                    V.tensor_copy(y_v[3][:, :, t * P:(t + 1) * P], ps[:, 2 + t % 2, :].rearrange("p (b n) -> p b n", b=FB)
                                  ).then_inc(*S("o_out", l).by(1))
                st.leave()
                pa = merge_parts(l)
                g = 0
                for half in range(2):
                    for i in range(NBR):
                        for j in range(FB):
                            dve.wait_ge(*S("z_gate", l).at(g + 1))
                            dve.wait_ge(*pa.of(B_MERGE + 2 * (half * NBR + i) + 1, j))
                            p_, s_ = result(4 * (g % 2) + 2, mg_s[:, g % 2, :])
                            z = zT[:, half * FB + j, :]
                            if i == 0:
                                V.tensor_tensor(even(z) if ctx_out else z[:, 0:LAT], p_, s_, ALU.mult).then_inc(*S("z_part", l).by(1))
                            else:
                                t_ = mg_t[:, g % 2, :]
                                V.tensor_tensor(even(t_) if ctx_out else t_[:, 0:LAT], p_, s_, ALU.mult
                                                ).then_inc(*S("z_part", l).by(1))
                                dve.wait_ge(*S("z_part", l).at(g + 1))
                                own.wait()
                                own(V.tensor_tensor(z[:, 0:nt], z[:, 0:nt], t_[:, 0:nt], ALU.add))
                            g += 1
                st.leave()
                op = out_parts(l)
                dve.wait_ge(*S("rows1_in", l).at(64))
                dve.wait_ge(*S("x1_in", l).at(16 * full))

                def affine(x, row_g, row_b, done):
                    own(V.tensor_tensor(x, x, row_g, ALU.mult))
                    own.wait()
                    done(V.tensor_tensor(x, x, row_b, ALU.add))

                for t in range(full):
                    for half in range(2):
                        dve.wait_ge(*op.of(B_OUT + half, t))
                    x, tmp = x1[:, t, :], t1[:, t % 2, :]
                    V.tensor_tensor(tmp, psf[:, t % 2 * D:(t % 2 + 1) * D], rows1[:, t // TL, :], ALU.mult
                                    ).then_inc(*S("p_y", l).by(1))
                    dve.wait_ge(*S("p_y", l).at(t + 1))
                    own(V.scalar_tensor_tensor(x, x, ALPHA, tmp, ALU.mult, ALU.add))
                    own.wait()
                    own(standardise(x, x, stat[:, 0, :], S("p_var", l), S("p_std", l), 2 * t + 1))
                    own.wait()
                    affine(x, rows1[:, 2, :], rows1[:, 3, :], own)
                    own.wait()
                    standardise(x, xn[:, t * D:(t + 1) * D], stat[:, 1, :], S("p_var", l), S("p_std", l), 2 * t + 2
                                ).then_inc(*S("xn", l).by(1))
                st.leave()
                dve.wait_ge(*S("r_logits", l).at(1))
                lg = ps[:, 0, 0:full * E].rearrange("p (t e) -> p t e", t=full)
                af = aff[:, 0:full, :]

                def over_e(v):
                    return v.unsqueeze(2).to_broadcast([P, full, E])

                own(V.tensor_reduce(rsm[:, 0, 0:full], lg, AX, ALU.max))
                own.wait()
                V.tensor_tensor(af, lg, over_e(rsm[:, 0, 0:full]), ALU.subtract).then_inc(*S("r_cent", l).by(1))
                dve.wait_ge(*S("r_exp", l).at(1))
                own(V.tensor_reduce(rsm[:, 1, 0:full], af, AX, ALU.add))
                own.wait()
                own(V.reciprocal(rsm[:, 2, 0:full], rsm[:, 1, 0:full]))
                own.wait()
                V.tensor_tensor(af, af, over_e(rsm[:, 2, 0:full]), ALU.mult).then_inc(*S("r_aff", l).by(1))
                dve.wait_ge(*S("r_affT", l).at(1))
                own(V.tensor_copy(affR[0:E, 0:nt], psf[0:E, 2 * 512:2 * 512 + nt]))
                own(V.tensor_copy(left[0:E, 0:nt], psf[0:E, 2 * 512:2 * 512 + nt]))
                own.wait()
                for a, b, cap in ((0, LAT, CAPL), (LAT, TOK, CAPC))[:2 if ctx_out else 1]:
                    for _ in range(cap // 8):
                        own(V.max(top8[0:E, :], left[0:E, a:b]))
                        own.wait()
                        own(V.match_replace(left[0:E, a:b], top8[0:E, :], left[0:E, a:b], -1.0))
                        own.wait()
                own(V.tensor_scalar(left[0:E, 0:nt], left[0:E, 0:nt], 0.0, None, ALU.is_lt))
                own.wait()
                for a, b in ((0, LAT), (LAT, TOK))[:2 if ctx_out else 1]:
                    own(V.tensor_tensor_scan(took[0:E, a:b], left[0:E, a:b], left[0:E, a:b], 0.0, ALU.add, ALU.max))
                own.wait()
                own(V.tensor_tensor(took[0:E, 0:nt], took[0:E, 0:nt], left[0:E, 0:nt], ALU.mult))
                own.wait()
                V.tensor_scalar(slotR[0:E, 0:nt], took[0:E, 0:nt], -1.0, None, ALU.add).then_inc(*S("slots", l).by(1))
                dve.wait_ge(*S("r_slotT", l).at(1))
                own(V.tensor_copy(slotT[:, 0:full, :], ps[:, 4, 0:full * E].rearrange("p (t e) -> p t e", t=full)))
                own.wait()
                for t in range(full):
                    cap = CAPL if t < TL else CAPC
                    V.tensor_tensor(pick_l[:, t, :, :] if t < TL else pick_c[:, t - TL, :, :],
                                    slot_row[:, 0:cap].unsqueeze(1).to_broadcast([P, E, cap]),
                                    slotT[:, t, :].unsqueeze(2).to_broadcast([P, E, cap]), ALU.is_equal)
                st.leave()
                st.leave()
                m = CAP if ctx_out else CAPL
                nload = 4 if ctx_out else 2
                r0e = l * LAYER_BLOCKS + B_EXP
                dve.wait_ge(*S("acc_zero", l).at(1))
                ncomb = 2 * full
                dve.drain().then_inc(*S("e_put", l).by(1))
                dve.drain().then_inc(*S("e_acc", l).by(1))
                with turns(dve, E // 2) as i:
                    for j in range(2):
                        dve.wait_ge(*S("pair_in", l).at(i * 32 * nload + 16 * nload * (j + 1)))
                        for a, b, r in ((0, LAT, slice(0, CAPL)), (LAT, TOK, slice(CAPL, CAP)))[:2 if ctx_out else 1]:
                            last = V.scalar_tensor_tensor(put[r, a:b], pair[r, 0, a:b], slot_col[r, :], pair[r, 1, a:b],
                                                          ALU.is_equal, ALU.mult)
                        last.then_inc(*S("e_put", l).by(1))
                        for half in range(2):
                            dve.wait_ge(*S("e_sil", l).at(i * 4 + 2 * j + half + 1))
                            dve.wait_ge(ring_used, i * 12 + (r0e + 6 * j + 2 * half + 2))
                            c = slice(half * NCH, (half + 1) * NCH)
                            V.tensor_tensor(hid[0:m, c], hid[0:m, c], ps[0:m, 2 * half + 1, :], ALU.mult
                                            ).then_inc(*S("e_hid", l).by(1))
                        for c in range(ncomb):
                            half, t = c // full, c % full
                            dve.wait_ge(*S("e_comb", l).at(i * 2 * ncomb + (ncomb * j + c + 2)))
                            a = acc[:, t, half * NCH:(half + 1) * NCH]
                            V.tensor_tensor(a, a, ps[:, c % 4, :], ALU.add).then_inc(*S("e_acc", l).by(1))
                st.leave()
                for t in range(full):
                    x, a = x1[:, t, :], acc[:, t, :]
                    own(V.tensor_tensor(a, a, rows2[:, t // TL, :], ALU.mult))
                    own.wait()
                    own(V.scalar_tensor_tensor(x, x, ALPHA, a, ALU.mult, ALU.add))
                    own.wait()
                    own(standardise(x, x, stat[:, 0, :], S("q_var", l), S("q_std", l), t + 1))
                    own.wait()
                    affine(x, rows2[:, 2, :], rows2[:, 3, :], lambda ins: ins.then_inc(*S("x2", l).by(1)))
                st.leave()

        for l in range(DEPTH):
            layer(l)
            for sem in sems.values():
                if isinstance(sem, Signal):
                    sem.next_layer()


def count_outs(l, order, j):
    return sum(c < tiles_out(l) for c in order[:j])


_DIRECT = ["x", "ctx", "w_mod", "b_mod", "attn_sink", "mlstm_gate_b", "w_branch", "w_gate", "w_out", "ln1_g", "ln1_b",
           "w_router", "w_exp_gate", "w_exp_up", "w_exp_down", "ln2_g", "ln2_b"]


def _layouts(inputs):
    a = {n: np.ascontiguousarray(inputs[n]) for n in _DIRECT}
    f = np.float32

    def col_major(v):
        return np.moveaxis(v.reshape(v.shape[:-1] + (-1, P)), -1, 0)

    a["cT"] = np.ascontiguousarray(np.stack([col_major(inputs["c"][0]), col_major(inputs["c_ctx"])], axis=-1))
    w = inputs["w_in"]
    o = {"qA": 0, "kA": 512, "vA": 640, "qB": 768, "kB": 1280, "vB": 1792, "ca": 2304, "cg": 2816, "qD": 3328,
         "kD": 3840, "vD": 4352, "oD": 4864, "g": 5376}
    blk = np.zeros((DEPTH, IN_BLOCKS, D, NCH), f)
    for i, name in ((0, "ca"), (1, "cg"), (2, "qA"), (4, "qB"), (5, "kB"), (6, "vB"), (7, "qD"), (8, "kD"), (9, "vD"),
                    (10, "oD")):
        blk[:, i] = w[:, :, o[name]:o[name] + NCH]
    for r in range(2):
        k = w[:, :, o["kA"] + r * HD:o["kA"] + (r + 1) * HD]
        blk[:, 3, :, 2 * r * HD:(2 * r + 1) * HD] = k
        blk[:, 3, :, (2 * r + 1) * HD:(2 * r + 2) * HD] = k
    blk[:, 3, :, 2 * P:3 * P] = w[:, :, o["vA"]:o["vA"] + P]
    blk[:, 3, :, 3 * P:3 * P + 16] = w[:, :, o["g"]:o["g"] + 16]
    a["w_in"] = np.ascontiguousarray(blk.reshape(DEPTH, IN_BLOCKS, KD, P, NCH).transpose(0, 1, 3, 2, 4))
    cc = np.concatenate([inputs["conv_w"].transpose(0, 2, 1), inputs["conv_b"][..., None],
                         inputs["conv_ln_g"][..., None], inputs["conv_ln_b"][..., None]], axis=-1)
    a["conv_c"] = np.ascontiguousarray(cc.reshape(DEPTH, FB, P, KS + 3).transpose(0, 2, 1, 3))
    a["b_gate"] = np.ascontiguousarray(inputs["b_gate"].reshape(DEPTH, NBR, KD, P).transpose(0, 3, 1, 2))
    rpb = inputs["na_rpb"]
    nr, ncol = rpb.shape[2], rpb.shape[3]
    reach, win = nr // 2, (ncol + 1) // 2
    bias = np.full((DEPTH, 2, GRID_W, HEADS, DROWS, GRID_W), NEG, f)
    for qc in range(GRID_W):
        c0 = min(max(qc - win // 2, 0), GRID_W - win)
        for par in range(2):
            for r in range(par, min(DROWS, nr + par)):
                bias[:, par, qc, :, r, c0:c0 + win] = rpb[:, :, r - par, c0 - qc + win - 1:c0 - qc + 2 * win - 1]
    a["bias"] = np.ascontiguousarray(bias.reshape(DEPTH, P, HEADS, DROWS * GRID_W))
    i, j = np.arange(P)[:, None], np.arange(P)[None, :]
    a["consts"] = np.concatenate([
        np.eye(P), np.ones((P, P)), i <= j, i >= j,
        np.where(j >= i, 0, NEG), np.zeros((P, P)), np.where(j <= i, 0, NEG)], axis=1).astype(f)
    slot = np.where(np.arange(P) < CAPL, np.arange(P), np.arange(P) - CAPL)
    a["iotas"] = np.concatenate([slot[:, None], np.broadcast_to(np.arange(CAPL), (P, CAPL))], axis=1).astype(f)
    half, nf = HD // 2, HD // 4
    inv = (f(10000.0) ** (-np.arange(nf, dtype=f) / f(nf))).astype(f)
    d = np.arange(P) % HD
    t = np.arange(LAT)
    pos = np.where(d[:, None] < half, t[None] // GRID_W, t[None] % GRID_W).astype(f)
    ang = pos * inv[d % nf][:, None]
    rot = np.zeros((P, P), f)
    for q in range(P):
        rot[q + nf if d[q] % half < nf else q - nf, q] = -1 if d[q] % half < nf else 1
    a["rope"] = np.concatenate([np.cos(ang), np.sin(ang), rot], axis=1).astype(f)
    return a


def kernel(**inputs):
    import concourse.bacc as _bacc
    from concourse.bass_utils import run_bass_kernel_spmd as _run
    inputs = {n: np.asarray(v) for n, v in inputs.items()}
    arrays = _layouts(inputs)
    nc = _bacc.Bacc("TRN2", target_bir_lowering=False, num_devices=1)
    args = {n: nc.dram_tensor(f"in_{n}", v.shape, mybir.dt.from_np(v.dtype), kind="ExternalInput").ap()
            for n, v in arrays.items()}
    out = nc.dram_tensor("out_x", (1, LAT, D), mybir.dt.float32, kind="ExternalOutput").ap()
    build(nc, args, out)
    r = _run(nc, [{f"in_{n}": v for n, v in arrays.items()}], core_ids=[0])
    return r.results[0]["out_x"]
```

```python
import concourse.bass as bass
from concourse import mybir
from contextlib import ExitStack, contextmanager
import numpy as np

P = 128
D = 1024
KD = D // P
DEPTH = 2
LAT, CTX = 512, 256
TOK = LAT + CTX
TL, TC = LAT // P, CTX // P
NT = TL + TC
GRID_W = 64
HD = 64
HEADS = 8
MH = 4
MU = 2 * MH
KS = 31
HALO = KS // 2
BW = 512
FB = BW // P
NBR = 4
E = 16
CAPL, CAPC = 2 * LAT // E, 2 * CTX // E
CAP = CAPL + CAPC
EPS = 1e-6
NEG = -1e30
ALPHA = float((2.0 * DEPTH) ** 0.25)
QSCALE = float(HD ** -0.5)
MSCALE = float(P ** -0.5)
RING = 4
TLAG, VLAG = 3, 4
NPROB, NSOFT = 5, 6
WB = 2048
QC = WB // KD
NCH = 512
DROWS = 16
LSEG, CSEG = LAT + 2 * HALO, CTX + 2 * HALO
AREA = 23072
MV = P + 1

MOD_BLOCKS = 6 * D // QC
IN_BLOCKS = 22
B_IN = MOD_BLOCKS
B_MERGE = B_IN + IN_BLOCKS
B_OUT = B_MERGE + 3 * 2 * NBR
B_EXP = B_OUT + 4
EXP_BLOCKS = 12
LAYER_BLOCKS = B_EXP + EXP_BLOCKS * E
MIX_SPLITS = IN_BLOCKS + 2 * 2 * NBR
BRANCHES = (1, 2, 3, 0)
S_CONV, S_D, S_O, S_MERGE = 10, 14, 20, 22


def expert_block(b):
    if b < 8:
        return ("w_exp_gate", "w_exp_up")[b // 2 % 2], b // 4 * NCH, b % 2
    return "w_exp_down", b % 2 * NCH, (b - 8) // 2


def split_block(q):
    return B_IN + q if q < IN_BLOCKS else B_MERGE + 3 * ((q - IN_BLOCKS) // 2) + (q - IN_BLOCKS) % 2


LAYER_SIGNALS = """
mod_bias_in params_in mod_row mod_out xhat x_in0 x_in1 conv_zero rope_in bias_in0 bias_in1 a_rcp a_scaled
a_max rows1_in router_in slots slots_out rows2_in acc_zero put_zero e_put pair_in xg x2 x_out mod_cols h_tmp h_hi h_done xhat_T
conv_glu rope_done rope_rot conv_sum conv_sq conv_sumsq a_exp a_scores a_probT a_turned a_out a_values m_cum
m_diag m_rows m_scores m_arg m_keys m_weights m_num m_mm m_kw m_state m_outer o_sig o_mm o_gated o_out
o_turned z_part p_y xn xn_hi xn_lo h2_tmp xn_T r_logits r_aff r_affT r_slotT g_out g_mm e_acc e_hid e_turned e_hH e_hL
e_yH e_yL e_comb var std conv_sig conv_cent conv_var conv_std conv_normed m_abs m_log m_exps m_arg2 m_gate
m_carried p_var p_std z_gate r_cent r_exp e_sil q_var q_std conv_part ab_part d_part ab_out d_out
merge_part out_part ya_out ya_in x1_out x1_in pt_in0 pt_in1
""".split()


def tiles_out(l):
    return NT if l < DEPTH - 1 else TL


def units(l):
    return [(kind, h, n) for kind in "AB" for h in range(HEADS) for n in range(tiles_out(l))]


def local_keys(kind, n):
    if n >= TL:
        return 0, 0
    if kind == "B":
        return 0, LAT
    return max(n - 1, 0) * P, min(n + 2, TL) * P


class Chain:

    def __init__(self, eng, sem):
        self.eng, self.sem, self.n, self.at = eng, sem, 0, None

    def __call__(self, ins):
        self.n += 1
        ins.then_inc(self.sem, 1)

    def wait(self, lag=0):
        self.eng.wait_ge(self.sem, self.n - lag if self.at is None else self.at + self.n - lag)


class Signal:
    turns = 1

    def __init__(self, sem):
        self.sem, self.before, self.now = sem, 0, 0

    def by(self, k):
        self.now += k * Signal.turns
        return self.sem, k

    def at(self, v):
        return self.sem, v + self.before

    def next_layer(self):
        self.before, self.now = self.before + self.now, 0


@contextmanager
def turns(eng, n):
    Signal.turns = n
    with eng.Fori(0, n) as i:
        yield i
    Signal.turns = 1


class Parts:

    def __init__(self, sem, ring_used, layer, order, count):
        self.early, self.place, n = sem, {}, 0
        self.ring_used, self.first = ring_used, layer * LAYER_BLOCKS
        for b, j in order:
            last = j == (count[b] if isinstance(count, dict) else count) - 1
            n += not last
            self.place[b, j] = None if last else n

    def by(self, b, j):
        return (self.ring_used, 1) if self.place[b, j] is None else self.early.by(1)

    def of(self, b, j):
        n = self.place[b, j]
        return (self.ring_used, self.first + b + 1) if n is None else self.early.at(n)


def build(nc, A, out):
    f32, f32r = mybir.dt.float32, mybir.dt.float32r
    ALU = mybir.AluOpType
    ACT = mybir.ActivationFunctionType
    AX = mybir.AxisListType.X
    ctx = ExitStack()
    with ctx:
        def sb(name, shape):
            return ctx.enter_context(nc.sbuf_tensor(name, shape, f32))

        sems = {n: Signal(ctx.enter_context(nc.semaphore(n))) for n in LAYER_SIGNALS}
        for n in ("stage_done", "ring_used", "const_in", "silu", "act_own", "dve_own", "split_h", "split_p", "split_v",
                  *(f"ring_in{i}" for i in range(RING))):
            sems[n] = ctx.enter_context(nc.semaphore(n))

        def S(name, l=None):
            assert (name in LAYER_SIGNALS) == (l is not None), name
            return sems[name]

        mod_d = nc.dram_tensor("mod_d", (DEPTH, 2, 6 * D), f32, kind="Internal").ap()
        x_d = nc.dram_tensor("x_d", (NT, P, D), f32, kind="Internal").ap()
        slot_d = nc.dram_tensor("slot_d", (DEPTH, 2, E, TOK), f32, kind="Internal").ap()
        x1_d = nc.dram_tensor("x1_d", (NT, P, D), f32, kind="Internal").ap()
        ya_d = nc.dram_tensor("ya_d", (P, FB * TOK), f32, kind="Internal").ap()

        raw = sb("raw", [P, RING, WB])
        part = ctx.enter_context(nc.sbuf_tensor("part", [P, 2, 2, WB], f32r))
        hx = ctx.enter_context(nc.sbuf_tensor("hx", [P, 2 * KD * TOK], f32r))
        area = sb("area", [P, AREA])
        consts = sb("consts", [P, 4 * P + 3 * P])
        s2T = sb("s2T", [P, KD, 2])
        iotas = sb("iotas", [P, 1 + CAPL])
        modc = sb("modc", [P, 4, KD, 2])
        conv_c = sb("conv_c", [P, FB, KS + 3])
        gate_b = sb("gate_b", [P, 4 * MH])
        mgate_b = sb("mgate_b", [P, NBR, KD])
        sink_b = sb("sink_b", [P, HEADS])
        ps = ctx.enter_context(nc.psum_tensor("ps", [P, 8, 512], f32))
        psf = ps[:, :, :].rearrange("p b n -> p (b n)")

        ident, ones, upper, lower = (consts[:, i * P:(i + 1) * P] for i in range(4))
        band = consts[:, 4 * P:7 * P]
        neg_ge, neg_le = band[:, 0:P], band[:, 2 * P:3 * P]
        slot_col, slot_row = iotas[:, 0:1], iotas[:, 1:1 + CAPL]

        def cut(t, at, *shape):
            n = int(np.prod(shape))
            assert at + n <= t.shape[1], (at, n, t.shape)
            v = t[:, at:at + n]
            if len(shape) == 2:
                v = v.rearrange("p (a b) -> p a b", a=shape[0])
            if len(shape) == 3:
                v = v.rearrange("p (a b c) -> p a b c", a=shape[0], b=shape[1])
            return v, at + n

        def parts_of(t, at, *shape):
            n = int(np.prod(shape))
            return cut(t, at, *shape)[0], cut(t, at + n, *shape)[0], at + 2 * n

        ys, work = area[:, 0:NBR * FB * TOK], area[:, NBR * FB * TOK:AREA]
        WORK = AREA - NBR * FB * TOK
        h_hi, h_lo, _ = parts_of(hx, 0, KD, TOK)
        xn_hi, xn_lo, _ = parts_of(hx, 0, NT, D)
        y_v = [cut(ys, i * FB * TOK, FB, TOK)[0] for i in range(NBR)]
        mod_row, o = cut(ys, 0, 6 * D)
        mod_bias, _ = cut(work, 0, 6 * D)
        xin, o = cut(work, 0, 2, D)
        xhat, o = cut(work, o, 2, D)
        htmp, o = cut(work, o, 2, KD, P)
        gates, oG = cut(work, 0, NT, 4 * MH)
        kA, o = cut(work, oG, 2, TOK)
        vA, o = cut(work, o, NT, P)
        kB = y_v[3]
        vB, _ = cut(ys, 2 * FB * TOK, NT, BW)
        rope_t, oc = cut(work, o, 2, LAT)
        rot, oc = cut(work, oc, P)
        rope_s, oc = cut(work, oc, 2, LAT)
        bias, oc = cut(work, o, 2, DROWS * GRID_W)
        prob, oc = cut(work, oc, NPROB, TOK)
        probT, oc = cut(work, oc, 2, TOK)
        soft, oc = cut(work, oc, NSOFT, 8)
        kD, o = cut(work, oG, MH, TOK)
        vD, oD = cut(work, o, NT, MH, MV)
        cpad, oc = cut(work, oD, FB, LSEG + CSEG)
        cstd, oc = cut(work, oc, TOK)
        csg = cstd
        csq, _ = cut(work, oD, 2, TOK)
        hD, _ = cut(ys, 0, NT, BW)
        mA, o = cut(work, oD, MU, P)
        mB, o = cut(work, o, MU, P)
        mC, o = cut(work, o, MU, MV)
        cst, o = cut(work, o, MU, MV)
        mcols = sb("mcols", [P, 2 * NT * MU])
        ig_c, o2 = cut(mcols, 0, NT, MU)
        lf_c, _ = cut(mcols, o2, NT, MU)
        lt_c, o = cut(work, o, NT, MU)
        u_c, o = cut(work, o, NT, MU)
        F_c, o = cut(work, o, NT, MU)
        FL_c, o = cut(work, o, NT, MU)
        m_c, o = cut(work, o, MU)
        cm_c, o = cut(work, o, 2, MU)
        M_c, o = cut(work, o, 2, MU)
        nM_c, o = cut(work, o, MU)
        ex_in, o = cut(work, o, 4, MU)
        ex_c, o = cut(work, o, 4, MU)
        den, o = cut(work, o, 3, MU)
        sig_o, _ = cut(work, oG, 2, QC)
        zT, _ = cut(work, WORK - KD * TOK, KD, TOK)
        mg_s, o = cut(work, 0, 2, TOK)
        mg_t, o = cut(work, o, 2, TOK)
        assert o <= WORK - KD * TOK
        rows1, o = cut(ys, 0, 4, D)
        t1, o = cut(ys, o, 2, D)
        xt, o = cut(ys, o, 2, D)
        xnt, o = cut(ys, o, 2, D)
        h2t, _ = cut(work, 0, 2, KD, P)
        wr, _ = cut(work, 2 * D, KD, E)
        aff, o = cut(work, 6144, NT, E)
        slotT, o = cut(work, o, NT, E)
        rsm, o = cut(work, o, 4, NT)
        affR, o = cut(work, o, TOK)
        left, o = cut(work, o, TOK)
        took, o = cut(work, o, TOK)
        slotR, o = cut(work, o, TOK)
        top8, o = cut(work, o, 8)
        pick_l = [part[:, 0, g, :].rearrange("p (t e c) -> p t e c", t=TL, e=8) for g in range(2)]
        pick_c = part[:, 1, 0, 0:TC * E * CAPC].rearrange("p (t e c) -> p t e c", t=TC, e=E)
        xgT, _ = cut(ys, 0, KD, E, CAP)
        acc, o = cut(work, 0, NT, D)
        pair, o = cut(work, o, 2, TOK)
        hid, o = cut(work, o, D)
        vscr, o = cut(work, o, TOK)
        val, o = cut(work, o, 2)
        assert o <= WORK
        put, o = cut(hx, 0, TOK)
        y_hi, y_lo, o = parts_of(hx, o, D)
        hd_hi, hd_lo, o = parts_of(hx, o, KD, CAP)
        xg_hi, xg_lo, o = parts_of(hx, o, KD, CAP)
        part3, o = cut(hx, o, 2, WB)

        def expert_part(q, which):
            v = part[:, q % 3, which, :] if q % 3 < 2 else part3[:, which, :]
            return v.rearrange("p (k n) -> p k n", k=4)

        x2v, o = cut(ys, 0, NT, D)
        rows2, o = cut(ys, o, 4, D)
        stat = sb("stat", [P, 2, 18])

        stage = S("stage_done")
        ring_in = [S(f"ring_in{i}") for i in range(RING)]
        ring_used = S("ring_used")

        def conv_parts(l):
            order = [(B_IN + S_CONV + 2 * c + b, j) for c in range(2) for j in range(2) for b in range(2)]
            return Parts(S("conv_part", l), ring_used, l, order, 2)

        AB_GROUPS = [(b, j, 2, "f", "qA", 2 * b + j) for b in range(2) for j in range(2)]
        AB_GROUPS += [(2, j, 2, "f", "kA", j) for j in range(2)] + [(3, t, NT, "t", "vA", t) for t in range(NT)]
        AB_GROUPS += [(4 + b, j, 2, "f", "qB", 2 * b + j) for b in range(2) for j in range(2)]
        AB_GROUPS += [(6 + b, j, 2, "f", "kB", 2 * b + j) for b in range(2) for j in range(2)]
        AB_GROUPS += [(8 + b, t, NT, "t", "vB", (t, b)) for b in range(2) for t in range(NT)]
        D_GROUPS = [(S_D + b, j, 2, "f", "qD", 2 * b + j) for b in range(2) for j in range(2)]
        D_GROUPS += [(S_D + 2 + b, j, 2, "f", "kD", 2 * b + j) for b in range(2) for j in range(2)]
        D_GROUPS += [(S_D + 4 + b, t, NT, "t", "vD", (t, b)) for b in range(2) for t in range(NT)]

        def group_parts(name, l, groups):
            return Parts(S(name, l), ring_used, l, [(B_IN + g[0], g[1]) for g in groups],
                         {B_IN + g[0]: g[2] for g in groups})

        def merge_parts(l):
            order = [(B_MERGE + 3 * i + b, j) for i in range(2 * NBR) for j in range(FB) for b in (j // 2, 2)]
            return Parts(S("merge_part", l), ring_used, l, [(b, j % 2 if (b - B_MERGE) % 3 < 2 else j) for b, j in order],
                         {b: 2 if (b - B_MERGE) % 3 < 2 else FB for b, _ in order})

        def gate_part(it, j):
            return B_MERGE + 3 * it + j // 2, j % 2

        def out_parts(l):
            order = [(B_OUT + c, t) for t in range(tiles_out(l)) for c in range(4)]
            return Parts(S("out_part", l), ring_used, l, order, tiles_out(l))

        class Split:

            def __init__(self, eng, which):
                self.eng, self.which = eng, which

            def mixers_to(self, l, end):
                key = "split" + self.which
                for q in range(state.get((key, l), 0), min(end, MIX_SPLITS)):
                    n = l * LAYER_BLOCKS + split_block(q)
                    if self.which == "hi":
                        self.eng.wait_ge(ring_in[n % RING], 16 * (n // RING + 1))
                        if q >= 2:
                            self.eng.wait_ge(ring_used, l * LAYER_BLOCKS + split_block(q - 2) + 1)
                        nc.scalar.activation(part[:, q % 2, 0, :], raw[:, n % RING, :], ACT.Copy).then_inc(S("split_h"), 1)
                    else:
                        self.eng.wait_ge(S("split_h"), l * (MIX_SPLITS + EXP_BLOCKS * E) + q + 1)
                        nc.gpsimd.tensor_tensor(part[:, q % 2, 1, :], raw[:, n % RING, :],
                                                part[:, q % 2, 0, :].bitcast(f32), ALU.subtract).then_inc(S("split_p"), 1)
                    state[key, l] = q + 1

        block = ctx.enter_context(nc.Block())

        class Stages:

            def __init__(self, eng):
                self.eng, self.k = eng, 0

            def leave(self):
                self.eng.drain().then_inc(stage, 1)
                self.k += 1
                self.eng.wait_ge(stage, 4 * self.k)

        state = {}

        def layer(l):
            @block.sync
            def _(sp):
                n = l * LAYER_BLOCKS
                h0, p0, v0 = l * (MIX_SPLITS + EXP_BLOCKS * E), l * MIX_SPLITS, l * EXP_BLOCKS * E
                splits = {split_block(q): q for q in range(MIX_SPLITS)}

                def slot_free(m):
                    b = m - RING
                    if b < 0:
                        if l:
                            sp.wait_ge(S("split_v"), v0 + RING + b + 1)
                    elif b in splits:
                        sp.wait_ge(S("split_p"), p0 + splits[b] + 1)
                    elif b < B_EXP:
                        sp.wait_ge(ring_used, l * LAYER_BLOCKS + b + 1)

                def load(src, k, cols):
                    nonlocal n
                    slot_free(n - l * LAYER_BLOCKS)
                    dst = raw[:, n % RING, :]
                    if k:
                        dst = dst.rearrange("p (k n) -> p k n", k=k)
                        src = src[:, cols:cols + WB // k].rearrange("(k p) n -> p k n", p=P)
                    sp.dma_start(dst, src).then_inc(ring_in[n % RING], 16)
                    n += 1

                for c in range(MOD_BLOCKS):
                    load(A["w_mod"][l], KD, QC * c)
                for c in range(IN_BLOCKS):
                    load(A["w_in"][l, c], 0, 0)
                for half in range(2):
                    for i in BRANCHES:
                        for c in range(2):
                            load(A["w_gate"][l], KD, i * D + half * NCH + c * QC)
                        load(A["w_branch"][l, i], FB, half * NCH)
                for c in range(4):
                    load(A["w_out"][l], KD, c * QC)
                assert EXP_BLOCKS * 2 % RING == 0
                n0 = n
                sp.wait_ge(ring_used, l * LAYER_BLOCKS + B_EXP)
                with sp.Fori(0, E // 2) as i:
                    for j in range(2 * EXP_BLOCKS):
                        name, c, kh = expert_block(j % EXP_BLOCKS)
                        sp.wait_ge(S("split_v"), i * 2 * EXP_BLOCKS + (v0 + j + 1))
                        src = A[name][l, bass.ds(i * 2 + j // EXP_BLOCKS, 1), kh * NCH:(kh + 1) * NCH, c:c + NCH]
                        sp.dma_start(raw[:, (n0 + j) % RING, :].rearrange("p (k n) -> p k n", k=4),
                                     src.rearrange("a (k p) n -> p (a k) n", p=P)).then_inc(ring_in[(n0 + j) % RING], 16)
                n += EXP_BLOCKS * E
                assert n == (l + 1) * LAYER_BLOCKS

            @block.gpsimd
            def _(pool):
                st = state.setdefault("pool", Stages(pool))
                load = nc.gpsimd.dma_start
                split = Split(pool, "lo")

                def x_tile(l, t):
                    if l:
                        return x_d[t]
                    return A["x"][0, t * P:(t + 1) * P, :] if t < TL else A["ctx"][0, (t - TL) * P:(t - TL + 1) * P, :]

                for dst, name in ((consts[:, :], "consts"), (s2T[:, :, :], "cT"), (iotas[:, :], "iotas"))[:3 if l == 0 else 0]:
                    load(dst, A[name]).then_inc(S("const_in"), 16)
                full = tiles_out(l)
                load(mod_bias[0:2, :], A["b_mod"][l:l + 1, :].to_broadcast([2, 6 * D])).then_inc(*S("mod_bias_in", l).by(16))
                load(conv_c[:, :, :], A["conv_c"][l]).then_inc(*S("params_in", l).by(16))
                load(gate_b[:, :], A["mlstm_gate_b"][l:l + 1, :].to_broadcast([P, 4 * MH])).then_inc(*S("params_in", l).by(16))
                load(sink_b[:, :], A["attn_sink"][l:l + 1, :].to_broadcast([P, HEADS])).then_inc(*S("params_in", l).by(16))
                load(mgate_b[:, :, :], A["b_gate"][l]).then_inc(*S("params_in", l).by(16))
                pool.wait_ge(*S("mod_row", l).at(MOD_BLOCKS))
                load(mod_d[l], mod_row[0:2, :]).then_inc(*S("mod_out", l).by(16))
                pool.wait_ge(*S("mod_out", l).at(16))
                pool.wait_ge(*S("params_in", l).at(64))
                st.leave()
                for t in range(NT):
                    if t >= 2:
                        pool.wait_ge(*S("xhat", l).at(t - 1))
                    load(xin[:, t % 2, :], x_tile(l, t)).then_inc(*S(f"x_in{t % 2}", l).by(16))
                st.leave()
                load(rope_t, A["rope"][:, 0:2 * LAT].rearrange("p (a n) -> p a n", a=2)).then_inc(*S("rope_in", l).by(16))
                load(rot, A["rope"][:, 2 * LAT:2 * LAT + P]).then_inc(*S("rope_in", l).by(16))
                split.mixers_to(l, S_CONV + 2)
                pool.wait_ge(*S("rope_in", l).at(32))
                st.leave()
                st.leave()
                def load_bias(h):
                    load(bias[:, h % 2, :], A["bias"][l, :, h, :]).then_inc(*S(f"bias_in{h % 2}", l).by(16))

                load_bias(0)
                load_bias(1)
                for u, (kind, h, n) in enumerate(units(l)):
                    lo, hi = local_keys(kind, n)
                    nk = hi - lo + CTX
                    pool.wait_ge(*S("a_rcp", l).at(u + 1))
                    nc.gpsimd.tensor_scalar(prob[:, u % NPROB, 0:nk], prob[:, u % NPROB, 0:nk], soft[:, u % NSOFT, 6:7],
                                            None, ALU.mult).then_inc(*S("a_scaled", l).by(1))
                    if kind == "B" and n == 0 and 1 <= h < HEADS - 1:
                        pool.wait_ge(*S("a_max", l).at(u))
                        load_bias(h + 1)
                st.leave()
                nc.gpsimd.memset(cpad, 0.0).then_inc(*S("conv_zero", l).by(1))
                load(ya_d, ys[:, 0:FB * TOK]).then_inc(*S("ya_out", l).by(16))
                split.mixers_to(l, S_D + 2)
                pool.wait_ge(*S("ya_out", l).at(16))
                st.leave()
                split.mixers_to(l, S_O + 2)
                st.leave()
                st.leave()
                st.leave()
                split.mixers_to(l, S_MERGE + 2)
                st.leave()
                load(ys[:, 0:FB * TOK], ya_d).then_inc(*S("ya_in", l).by(16))
                split.mixers_to(l, MIX_SPLITS)
                st.leave()
                for v, src in enumerate((mod_d[l, 0:1, 2 * D:3 * D], mod_d[l, 1:2, 2 * D:3 * D],
                                         A["ln1_g"][l:l + 1, :], A["ln1_b"][l:l + 1, :])):
                    load(rows1[:, v, :], src.to_broadcast([P, D])).then_inc(*S("rows1_in", l).by(16))
                load(wr, A["w_router"][l].rearrange("(k p) e -> p k e", p=P)).then_inc(*S("router_in", l).by(16))
                for t in range(full + 1):
                    if t < full:
                        if t >= 2:
                            pool.wait_ge(*S("x1_out", l).at(16 * (t - 1)))
                        load(xt[:, t % 2, :], x_tile(l, t)).then_inc(*S(f"pt_in{t % 2}", l).by(16))
                    if t:
                        pool.wait_ge(*S("xn", l).at(t))
                        load(x1_d[t - 1], xt[:, (t - 1) % 2, :]).then_inc(*S("x1_out", l).by(16))
                pool.wait_ge(*S("x1_out", l).at(16 * full))
                st.leave()
                pool.wait_ge(*S("slots", l).at(1))
                for v, row in enumerate((slotR, affR)):
                    load(slot_d[l, v, :, 0:full * P], row[0:E, 0:full * P]).then_inc(*S("slots_out", l).by(16))
                pool.wait_ge(*S("slots_out", l).at(32))
                st.leave()
                st.leave()
                nc.gpsimd.memset(acc, 0.0).then_inc(*S("acc_zero", l).by(1))
                with turns(pool, E // 2) as i:
                    for j in range(2):
                        e = i * 2 + j
                        pool.wait_ge(ring_used, i * 2 * EXP_BLOCKS + (l * LAYER_BLOCKS + B_EXP + EXP_BLOCKS * j - 4))
                        src = xgT[:, :, bass.ds(e, 1), :].rearrange("p k a c -> p k (a c)")
                        nc.gpsimd.tensor_copy(xg_hi, src).then_inc(*S("xg", l).by(1))
                        pool.drain()
                        nc.gpsimd.tensor_tensor(xg_lo, src, xg_hi.bitcast(f32), ALU.subtract
                                                ).then_inc(*S("xg", l).by(1))
                        pool.wait_ge(*S("e_put", l).at(i * 2 + j + 1))
                        for v in range(2):
                            load(pair[0:CAPL, v, 0:LAT], slot_d[l, v, bass.ds(e, 1), 0:LAT].to_broadcast([CAPL, LAT])
                                 ).then_inc(*S("pair_in", l).by(16))
                            if full == NT:
                                load(pair[CAPL:CAP, v, LAT:TOK],
                                     slot_d[l, v, bass.ds(e, 1), LAT:TOK].to_broadcast([CAPC, CTX])
                                     ).then_inc(*S("pair_in", l).by(16))
                pool.wait_ge(*S("xg", l).at(2 * E))
                for v, src in enumerate((mod_d[l, 0:1, 5 * D:6 * D], mod_d[l, 1:2, 5 * D:6 * D],
                                         A["ln2_g"][l:l + 1, :], A["ln2_b"][l:l + 1, :])):
                    load(rows2[:, v, :], src.to_broadcast([P, D])).then_inc(*S("rows2_in", l).by(16))
                for t in range(full):
                    load(x2v[:, t, :], x1_d[t]).then_inc(*S("x1_in", l).by(16))
                st.leave()
                for t in range(full):
                    pool.wait_ge(*S("x2", l).at(t + 1))
                    dst = x_d[t] if l < DEPTH - 1 else out[0, t * P:(t + 1) * P, :]
                    load(dst, x2v[:, t, :]).then_inc(*S("x_out", l).by(16))
                pool.wait_ge(*S("x_out", l).at(16 * full))
                st.leave()

            @block.tensor
            def _(pe):
                st = state.setdefault("pe", Stages(pe))
                mm = nc.tensor.matmul
                n = l * LAYER_BLOCKS
                if l == 0:
                    pe.wait_ge(S("const_in"), 48)
                    pe.wait_ge(S("silu"), 1)

                taken = 0
                h0, p0, v0 = l * (MIX_SPLITS + EXP_BLOCKS * E), l * MIX_SPLITS, l * EXP_BLOCKS * E

                def take(k=KD):
                    nonlocal n
                    pe.wait_ge(ring_in[n % RING], 16 * (n // RING + 1))
                    n += 1
                    return raw[:, (n - 1) % RING, :].rearrange("p (k n) -> p k n", k=k)

                def take_split():
                    nonlocal n, taken
                    pe.wait_ge(S("split_p"), p0 + taken + 1)
                    n, taken = n + 1, taken + 1
                    return [part[:, (taken - 1) % 2, v, :].rearrange("p (k n) -> p k n", k=KD) for v in range(2)]

                def passes(dst, pairs):
                    for i, (a, b) in enumerate(pairs):
                        last = mm(dst, a, b, start=i == 0, stop=i == len(pairs) - 1)
                    return last

                def feature_major(bank, w, c, toks):
                    for a, b, bk in toks:
                        last = passes(ps[:, bank + bk, 0:b - a],
                                      [(w[u][:, k, c:c + P], h[:, k, a:b]) for k in range(KD)
                                       for u, h in ((0, h_hi), (0, h_lo), (1, h_hi))])
                    return last

                def token_major(dst, w, c0, c1, t):
                    return passes(dst, [(h[:, k, t * P:(t + 1) * P], w[u][:, k, c0:c1]) for k in range(KD)
                                        for h, u in ((h_hi, 0), (h_hi, 1), (h_lo, 0))])

                full = tiles_out(l)
                even = [(0, TOK // 2, 0), (TOK // 2, TOK, 1)]
                some = even if full == NT else [(0, LAT, 0)]
                for c in range(MOD_BLOCKS):
                    w = take()
                    if c >= 2:
                        pe.wait_ge(*S("mod_row", l).at(c - 1))
                    passes(ps[0:2, c % 2, 0:QC], [(s2T[:, k, :], w[:, k, :]) for k in range(KD)]).then_inc(ring_used, 1)
                pe.wait_ge(*S("mod_row", l).at(MOD_BLOCKS))
                for v, row in enumerate((0, 1, 3, 4)):
                    for k in range(KD):
                        o = (v * KD + k) * 2
                        last = nc.tensor.transpose(ps[:, 2, o:o + 2], mod_row[0:2, row * D + k * P:row * D + (k + 1) * P],
                                                   ident[0:2, 0:2])
                last.then_inc(*S("mod_cols", l).by(1))
                st.leave()
                for t in range(NT):
                    pe.wait_ge(*S("xhat", l).at(t + 1))
                    if t >= 2:
                        pe.wait_ge(*S("h_tmp", l).at(t - 1))
                    for k in range(KD):
                        last = nc.tensor.transpose(psf[:, t % 2 * D + k * P:t % 2 * D + (k + 1) * P],
                                                   xhat[:, t % 2, k * P:(k + 1) * P], ident)
                    last.then_inc(*S("xhat_T", l).by(1))
                st.leave()
                def project(name, groups, done):
                    pa = group_parts(name, l, groups)
                    block, w = None, None
                    for g, (b, j, _, kind, what, _) in enumerate(groups):
                        if b != block:
                            block, w = b, take_split()
                        if g >= 4:
                            pe.wait_ge(*done.at(g - 3))
                        bank = 2 * (g % 4)
                        if kind == "f":
                            last = feature_major(bank, w, j * P, some if what[0] == "q" else even)
                        else:
                            last = token_major(ps[:, bank, 0:P + 4 * MH] if what == "vA" else ps[:, bank, 0:QC],
                                               w, 0, P + 4 * MH if what == "vA" else QC, j)
                        last.then_inc(*pa.by(B_IN + b, j))

                project("ab_part", AB_GROUPS, S("ab_out", l))
                st.leave()
                for j in range(6):
                    if j >= 2:
                        pe.wait_ge(*S("rope_done", l).at(j - 1))
                    src = y_v[0][:, j, 0:LAT] if j < FB else kA[:, j - FB, 0:LAT]
                    mm(ps[:, j % 2, :], rot, src, start=True, stop=True).then_inc(*S("rope_rot", l).by(1))
                st.leave()
                us = units(l)
                for s in range(len(us) + VLAG):
                    if s < len(us):
                        kind, h, t = us[s]
                        hp = h % 2 * HD
                        lo, hi = local_keys(kind, t)
                        if s >= 2:
                            pe.wait_ge(*S("a_exp", l).at(s - 1))
                        q = y_v["AB".index(kind)][hp:hp + HD, h // 2, t * P:(t + 1) * P]
                        k = kA[hp:hp + HD, h // 4, :] if kind == "A" else kB[hp:hp + HD, h // 2, :]
                        if hi > lo:
                            mm(ps[:, 2 * (s % 2), 0:hi - lo], q, k[:, lo:hi], start=True, stop=True)
                        mm(ps[:, 2 * (s % 2) + 1, 0:CTX], q, k[:, LAT:TOK], start=True, stop=True).then_inc(*S("a_scores", l).by(1))
                    if TLAG <= s < len(us) + TLAG:
                        u = s - TLAG
                        lo, hi = local_keys(us[u][0], us[u][2])
                        pe.wait_ge(*S("a_scaled", l).at(u + 1))
                        if u >= 1:
                            pe.wait_ge(*S("a_probT", l).at(u))
                        for b in range((hi - lo + CTX) // P):
                            last = nc.tensor.transpose(psf[:, 4 * 512 + b * P:4 * 512 + (b + 1) * P],
                                                       prob[:, u % NPROB, b * P:(b + 1) * P], ident)
                        last.then_inc(*S("a_turned", l).by(1))
                    if s >= VLAG:
                        u = s - VLAG
                        kind, h, t = us[u]
                        lo, hi = local_keys(kind, t)
                        tiles = list(range(lo // P, hi // P)) + list(range(TL, NT))
                        pe.wait_ge(*S("a_probT", l).at(u + 1))
                        if u >= 2:
                            pe.wait_ge(*S("a_out", l).at(u - 1))
                        for b, kt in enumerate(tiles):
                            v = vA[:, kt, h // 4 * HD:h // 4 * HD + HD] if kind == "A" else vB[:, kt, h * HD:(h + 1) * HD]
                            last = mm(ps[0:HD, 6 + u % 2, 0:P], v, probT[:, u % 2, b * P:(b + 1) * P],
                                      start=b == 0, stop=b == len(tiles) - 1)
                        last.then_inc(*S("a_values", l).by(1))
                st.leave()
                pa = conv_parts(l)
                toks = [(0, LAT, 0), (LAT, TOK, 1)] if full == NT else [(0, LAT, 0)]
                for j in range(FB):
                    if j % 2 == 0:
                        wa, wg = take_split(), take_split()
                    if j >= 2:
                        pe.wait_ge(*S("conv_glu", l).at(j - 1))
                    b = B_IN + S_CONV + j // 2 * 2
                    feature_major(4 * (j % 2), wa, j % 2 * P, toks).then_inc(*pa.by(b, j % 2))
                    feature_major(4 * (j % 2) + 2, wg, j % 2 * P, toks).then_inc(*pa.by(b + 1, j % 2))
                st.leave()
                project("d_part", D_GROUPS, S("d_out", l))
                st.leave()
                cuts = even if full == NT else [(0, LAT, 0)]
                for a, b, bk in cuts:
                    last = passes(ps[:, 2 + bk, 0:b - a], [(ones, y_v[2][:, j, a:b]) for j in range(FB)])
                last.then_inc(*S("conv_sum", l).by(1))
                for j in range(FB):
                    pe.wait_ge(*S("conv_sq", l).at(j + 1))
                    for a, b, bk in cuts:
                        last = mm(ps[:, 4 + bk, 0:b - a], ones, csq[:, j % 2, a:b], start=j == 0, stop=j == FB - 1)
                    last.then_inc(*S("conv_sumsq", l).by(1))
                st.leave()
                for d, tri in enumerate((upper, lower)):
                    mm(ps[:, 0, d * NT * MH:(d + 1) * NT * MH], tri, lf_c[:, :, d * MH:(d + 1) * MH], start=True, stop=True)
                mm(ps[:, 1, 0:NT * MU], ones, lf_c[:, :, :], start=True, stop=True).then_inc(*S("m_cum", l).by(1))
                fwd, bwd = [4, 5, 0, 1, 2, 3], [5, 4, 3, 2, 1, 0]
                for j in range(NT):
                    chunk = (fwd[j], bwd[j])
                    outs = fwd[j] < full
                    for half in range(2):
                        pe.wait_ge(*S("m_diag", l).at(2 * j + half + 1))
                        for g in range(2):
                            last = mm(ps[:, g, :], ones, mA[:, 4 * g:4 * g + 4, :], start=True, stop=True)
                        last.then_inc(*S("m_rows", l).by(1))
                    if outs:
                        for u in range(MU):
                            c = slice(chunk[u // MH] * P, (chunk[u // MH] + 1) * P)
                            last = mm(psf[:, 2 * 512 + u * P:2 * 512 + (u + 1) * P], kD[:, u % MH, c], y_v[3][:, u % MH, c],
                                      start=True, stop=True)
                        last.then_inc(*S("m_scores", l).by(1))
                    pe.wait_ge(*S("m_arg", l).at(j + 1))
                    for u in range(MU):
                        c = slice(chunk[u // MH] * P, (chunk[u // MH] + 1) * P)
                        last = nc.tensor.transpose(psf[:, u * P:(u + 1) * P], kD[:, u % MH, c], ident)
                    last.then_inc(*S("m_keys", l).by(1))
                    if outs:
                        pe.wait_ge(*S("m_weights", l).at(count_outs(l, fwd, j) + 1))
                        for d in range(2):
                            if d == 1:
                                pe.wait_ge(*S("m_num", l).at(2 * count_outs(l, fwd, j) + 1))
                            for q in range(MH):
                                u, o = d * MH + q, q % 2 * MV
                                mm(ps[:, 4 + q // 2, o:o + MV], mB[:, u, :], vD[:, chunk[d], q, :], start=True, stop=True)
                                last = mm(ps[:, 6 + q // 2, o:o + MV], y_v[3][:, q, chunk[d] * P:(chunk[d] + 1) * P],
                                          cst[:, u, :], start=True, stop=True)
                            last.then_inc(*S("m_mm", l).by(1))
                    pe.wait_ge(*S("m_kw", l).at(j + 1))
                    for d in range(2):
                        if d == 1:
                            pe.wait_ge(*S("m_state", l).at(2 * j + 1))
                        for q in range(MH):
                            o = q % 2 * MV
                            last = mm(ps[:, 2 + q // 2, o:o + MV], mA[:, d * MH + q, :], vD[:, chunk[d], q, :],
                                      start=True, stop=True)
                        last.then_inc(*S("m_outer", l).by(1))
                    pe.wait_ge(*S("m_state", l).at(2 * j + 2))
                st.leave()
                def turn_o(g):
                    half, t = g // full, g % full
                    pe.wait_ge(*S("o_gated", l).at(g + 1))
                    if g >= 2:
                        pe.wait_ge(*S("o_out", l).at(g - 1))
                    for b in range(2):
                        last = nc.tensor.transpose(ps[:, 2 + g % 2, b * P:(b + 1) * P],
                                                   hD[:, t, half * QC + b * P:half * QC + (b + 1) * P], ident)
                    last.then_inc(*S("o_turned", l).by(1))

                for half in range(2):
                    w = take_split()
                    for t in range(full):
                        g = half * full + t
                        if g >= 2:
                            pe.wait_ge(*S("o_gated", l).at(g - 1))
                        last = token_major(ps[:, g % 2, 0:QC], w, 0, QC, t)
                        last.then_inc(*(S("o_mm", l).by(1) if t < full - 1 else (ring_used, 1)))
                        if g:
                            turn_o(g - 1)
                turn_o(2 * full - 1)
                st.leave()
                pa = merge_parts(l)
                g = 0
                for it in range(2 * NBR):
                    i = BRANCHES[it % NBR]
                    if it == NBR - 1:
                        pe.wait_ge(*S("ya_in", l).at(16))
                    wb = None
                    for j in range(FB):
                        if j % 2 == 0:
                            wg = take_split()
                        if g >= 2:
                            pe.wait_ge(*S("z_part", l).at(g - 1))
                        feature_major(4 * (g % 2), wg, j % 2 * P, some).then_inc(*pa.by(*gate_part(it, j)))
                        if wb is None:
                            m_ = l * LAYER_BLOCKS + B_MERGE + 3 * it + 2
                            pe.wait_ge(ring_in[m_ % RING], 16 * (m_ // RING + 1))
                            wb = raw[:, m_ % RING, :].rearrange("p (k n) -> p k n", k=FB)
                        for a, b, bk in some:
                            last = passes(ps[:, 4 * (g % 2) + 2 + bk, 0:b - a],
                                          [(wb[:, k, j * P:(j + 1) * P], y_v[i][:, k, a:b]) for k in range(FB)])
                        last.then_inc(*pa.by(B_MERGE + 3 * it + 2, j))
                        g += 1
                    n += 1
                st.leave()
                op = out_parts(l)
                ws = [take() for _ in range(4)]
                pe.wait_ge(*S("router_in", l).at(16))
                for t in range(full + 2):
                    if t < full:
                        if t >= 2:
                            pe.wait_ge(*S("p_y", l).at(t - 1))
                        for c in range(4):
                            passes(psf[:, t % 2 * D + c * QC:t % 2 * D + (c + 1) * QC],
                                   [(zT[:, k, t * P:(t + 1) * P], ws[c][:, k, :]) for k in range(KD)]
                                   ).then_inc(*op.by(B_OUT + c, t))
                    if 1 <= t <= full:
                        pe.wait_ge(*S("xn", l).at(t))
                        if t >= 2:
                            pe.wait_ge(*S("h2_tmp", l).at(t - 1))
                        for k in range(KD):
                            last = nc.tensor.transpose(psf[:, 4 * 512 + k * P:4 * 512 + (k + 1) * P],
                                                       xnt[:, (t - 1) % 2, k * P:(k + 1) * P], ident)
                        last.then_inc(*S("xn_T", l).by(1))
                    if t >= 2:
                        pe.wait_ge(*S("h2_tmp", l).at(t - 1))
                        passes(ps[:, 6, (t - 2) * E:(t - 1) * E], [(h2t[:, t % 2, k, :], wr[:, k, :]) for k in range(KD)]
                               ).then_inc(*S("r_logits", l).by(1))
                st.leave()
                pe.wait_ge(*S("r_aff", l).at(1))
                for t in range(full):
                    last = nc.tensor.transpose(psf[0:E, 2 * 512 + t * P:2 * 512 + (t + 1) * P], aff[:, t, :], ident)
                last.then_inc(*S("r_affT", l).by(1))
                pe.wait_ge(*S("slots", l).at(1))
                for t in range(full):
                    last = nc.tensor.transpose(ps[:, 4, t * E:(t + 1) * E], slotR[0:E, t * P:(t + 1) * P], ident[0:E, 0:E])
                last.then_inc(*S("r_slotT", l).by(1))
                st.leave()
                g = 0
                for k in range(KD):
                    for c in range(3 if full == NT else 2):
                        if g >= 4:
                            pe.wait_ge(*S("g_out", l).at(g - 3))
                        ts = range(TL) if c < 2 else range(TC)
                        passes(ps[:, g % 4, :],
                               [(x[:, t if c < 2 else TL + t, k * P:(k + 1) * P],
                                 pick_l[c][:, t, :, :] if c < 2 else pick_c[:, t, :, :]) for t in ts for x in (xn_hi, xn_lo)]
                               ).then_inc(*S("g_mm", l).by(1))
                        g += 1
                st.leave()
                ncomb = 2 * full
                per = ncomb // 2 // 2
                n += EXP_BLOCKS * E
                pe.drain().then_inc(*S("e_comb", l).by(1))
                pe.wait_ge(*S("put_zero", l).at(1))

                def scatter(c, before):
                    half, t = c // full, c % full
                    pe.wait_ge(*S("e_acc", l).at(before + max(c - 1, 0)))
                    rr = slice(0, CAPL) if t < TL else slice(CAPL, CAP)
                    passes(ps[:, (4, 7)[c % 2], :], [(put[rr, t * P:(t + 1) * P], y[rr, half * NCH:(half + 1) * NCH])
                                                     for y in (y_hi, y_lo)]).then_inc(*S("e_comb", l).by(1))

                def turn_hidden(half, count):
                    pe.wait_ge(*S("e_hid", l).at(count))
                    for b in range(4):
                        last = nc.tensor.transpose(ps[:, (4, 7)[half], b * CAP:(b + 1) * CAP],
                                                   hid[0:CAP, (4 * half + b) * P:(4 * half + b + 1) * P], ident[0:CAP, 0:CAP])
                    last.then_inc(*S("e_turned", l).by(1))

                with turns(pe, E // 2) as i:
                    for j in range(2):
                        pe.wait_ge(*S("xg", l).at(i * 4 + 2 * j + 2))
                        for b in range(EXP_BLOCKS):
                            w = [expert_part(EXP_BLOCKS * j + b, v) for v in range(2)]
                            pe.wait_ge(S("split_v"), i * 2 * EXP_BLOCKS + (v0 + RING + EXP_BLOCKS * j + b + 1))
                            kh = expert_block(b)[2]
                            if b < 8:
                                bank, (x_hi, x_lo) = b // 2, (xg_hi, xg_lo)
                            else:
                                bank, (x_hi, x_lo) = 5 + b % 2, (hd_hi, hd_lo)
                                if b % 2 == 0:
                                    pe.wait_ge(*S("e_hL", l).at(i * 4 + 2 * j + kh + 1))
                            pairs = [(x[:, 4 * kh + k, :], w[u][:, k, :]) for k in range(4)
                                     for x, u in ((x_hi, 0), (x_hi, 1), (x_lo, 0))]
                            for a, (x, y) in enumerate(pairs):
                                last = mm(ps[0:CAP, bank, :], x, y, start=kh == 0 and a == 0, stop=kh == 1 and a == len(pairs) - 1)
                            last.then_inc(ring_used, 1)
                            if b < 4:
                                if b == 0:
                                    pe.wait_ge(*S("e_yL", l).at(i * 4 + 2 * j + 2))
                                for c in range(b * per, (b + 1) * per):
                                    scatter(c, i * 2 * ncomb + (ncomb * j + 1))
                            if b == 5:
                                pe.wait_ge(*S("e_acc", l).at(i * 2 * ncomb + (ncomb * j + ncomb + 1)))
                                turn_hidden(0, i * 4 + 2 * j + 1)
                            if b == 8:
                                turn_hidden(1, i * 4 + 2 * j + 2)
                pe.wait_ge(*S("e_yL", l).at(2 * E + 2))
                for c in range(ncomb):
                    scatter(c, E * ncomb + 1)
                st.leave()
                st.leave()

            @block.scalar
            def _(act):
                st = state.setdefault("act", Stages(act))
                fn = nc.scalar.activation
                own = state.setdefault("act_own", Chain(act, S("act_own")))
                split = Split(act, "hi")
                if l == 0:
                    act.wait_ge(S("const_in"), 48)
                    fn(s2T[:, :, :], s2T[:, :, :], ACT.Silu).then_inc(S("silu"), 1)
                full = tiles_out(l)
                ctx_out = full == NT

                def even(v):
                    return v.rearrange("p (a n) -> p a n", a=2)

                st.leave()
                def modulate(dst, t, base, v, done):
                    s = 0 if t < TL else 1
                    for k in range(KD):
                        last = fn(dst[:, k, :], psf[:, base + k * P:base + (k + 1) * P], ACT.Identity,
                                  bias=modc[:, v, k, s:s + 1], scale=modc[:, v + 1, k, s:s + 1])
                    last.then_inc(*done.by(1))

                for t in range(NT + 1):
                    if t < NT:
                        act.wait_ge(*S("var", l).at(t + 1))
                        fn(stat[:, t % 2, 15:16], stat[:, t % 2, 14:15], ACT.Sqrt).then_inc(*S("std", l).by(1))
                    if t:
                        u = t - 1
                        act.wait_ge(*S("xhat_T", l).at(u + 1))
                        if u >= 2:
                            act.wait_ge(*S("h_done", l).at(u - 1))
                        modulate(htmp[:, u % 2, :, :], u, u % 2 * D, 0, S("h_tmp", l))
                        act.wait_ge(*S("h_tmp", l).at(u + 1))
                        fn(h_hi[:, :, u * P:(u + 1) * P], htmp[:, u % 2, :, :], ACT.Copy).then_inc(*S("h_hi", l).by(1))
                split.mixers_to(l, 2)
                st.leave()

                def copies(name, groups, done):
                    pa = group_parts(name, l, groups)
                    for g, (b, j, count, _, what, idx) in enumerate(groups):
                        act.wait_ge(*pa.of(B_IN + b, j))
                        bank = 2 * (g % 4)
                        if what == "vA":
                            fn(vA[:, idx, :], ps[:, bank, 0:P], ACT.Copy)
                            last = fn(gates[:, idx, :], ps[:, bank, P:P + 4 * MH], ACT.Copy)
                        elif what == "vB":
                            t, half = idx
                            last = fn(vB[:, t, half * QC:(half + 1) * QC], ps[:, bank, 0:QC], ACT.Copy)
                        elif what == "vD":
                            t, half = idx
                            last = fn(vD[:, t, 2 * half:2 * half + 2, 0:P],
                                      ps[:, bank, 0:QC].rearrange("p (h n) -> p h n", h=2), ACT.Copy)
                        else:
                            dst = {"qA": y_v[0], "kA": kA, "qB": y_v[1], "kB": kB, "qD": y_v[3], "kD": kD}[what]
                            scale = QSCALE if what in ("qA", "qB") else MSCALE if what == "kD" else 1.0
                            if what[0] == "q" and not ctx_out:
                                last = fn(dst[:, idx, 0:LAT], ps[:, bank, :], ACT.Copy, scale=scale)
                            else:
                                last = fn(even(dst[:, idx, :]), ps[:, bank:bank + 2, 0:TOK // 2], ACT.Copy, scale=scale)
                        last.then_inc(*done.by(1))
                        if j == count - 1:
                            split.mixers_to(l, b + 3)

                copies("ab_part", AB_GROUPS, S("ab_out", l))
                st.leave()
                st.leave()
                us = units(l)
                for s in range(len(us) + TLAG):
                    if s < len(us):
                        kind, h, t = us[s]
                        lo, hi = local_keys(kind, t)
                        nl = hi - lo
                        sf = soft[:, s % NSOFT, :]
                        act.wait_ge(*S("a_max", l).at(s + 1))
                        if nl:
                            fn(prob[:, s % NPROB, 0:nl], prob[:, s % NPROB, 0:nl], ACT.Exp, bias=sf[:, 2:3], accum_out=sf[:, 3:4])
                        if kind == "A":
                            fn(sf[:, 5:6], sink_b[:, h:h + 1], ACT.Exp, bias=sf[:, 2:3])
                        fn(prob[:, s % NPROB, nl:nl + CTX], ps[:, 2 * (s % 2) + 1, 0:CTX], ACT.Exp, bias=sf[:, 2:3],
                           accum_out=sf[:, 4:5]).then_inc(*S("a_exp", l).by(1))
                    if s >= TLAG:
                        u = s - TLAG
                        lo, hi = local_keys(us[u][0], us[u][2])
                        act.wait_ge(*S("a_turned", l).at(u + 1))
                        if u >= 2:
                            act.wait_ge(*S("a_values", l).at(u - 1))
                        fn(probT[:, u % 2, 0:hi - lo + CTX], psf[:, 4 * 512:4 * 512 + hi - lo + CTX], ACT.Copy
                           ).then_inc(*S("a_probT", l).by(1))
                st.leave()
                pa = conv_parts(l)
                for j in range(FB):
                    act.wait_ge(*pa.of(B_IN + S_CONV + j // 2 * 2 + 1, j % 2))
                    if j >= 1:
                        act.wait_ge(*S("conv_glu", l).at(j))
                    b = 4 * (j % 2) + 2
                    last = fn(csg[:, 0:LAT], ps[:, b, :], ACT.Sigmoid)
                    if ctx_out:
                        last = fn(csg[:, LAT:TOK], ps[:, b + 1, 0:CTX], ACT.Sigmoid)
                    last.then_inc(*S("conv_sig", l).by(1))
                    if j % 2:
                        split.mixers_to(l, S_CONV + j // 2 * 2 + 4)
                st.leave()
                act.wait_ge(*S("m_abs", l).at(1))
                own(fn(lt_c[:, :, :], lt_c[:, :, :], ACT.Exp, scale=-1.0))
                own.wait()
                fn(lt_c[:, :, :], lt_c[:, :, :], ACT.Ln, bias=1.0).then_inc(*S("m_log", l).by(1))
                copies("d_part", D_GROUPS, S("d_out", l))
                st.leave()
                nt = TOK if ctx_out else LAT
                for j in range(FB):
                    act.wait_ge(*S("conv_cent", l).at(j + 1))
                    if j >= 2:
                        act.wait_ge(*S("conv_sumsq", l).at(j - 1))
                    fn(csq[:, j % 2, 0:nt], y_v[2][:, j, 0:nt], ACT.Square).then_inc(*S("conv_sq", l).by(1))
                act.wait_ge(*S("conv_var", l).at(1))
                fn(cstd[:, 0:nt], cstd[:, 0:nt], ACT.Sqrt).then_inc(*S("conv_std", l).by(1))
                for j in range(FB):
                    act.wait_ge(*S("conv_normed", l).at(j + 1))
                    fn(y_v[2][:, j, 0:nt], y_v[2][:, j, 0:nt], ACT.Silu, bias=conv_c[:, j, KS + 2:KS + 3],
                       scale=conv_c[:, j, KS + 1:KS + 2])
                st.leave()
                fwd = [4, 5, 0, 1, 2, 3]
                for j in range(NT):
                    outs = fwd[j] < full
                    act.wait_ge(*S("m_diag", l).at(2 * j + 2))
                    fn(ex_c[:, :, :], ex_in[:, :, :], ACT.Exp).then_inc(*S("m_exps", l).by(1))
                    if outs:
                        act.wait_ge(*S("m_arg2", l).at(count_outs(l, fwd, j) + 1))
                        fn(mB[:, :, :], mB[:, :, :], ACT.Exp).then_inc(*S("m_gate", l).by(1))
                    act.wait_ge(*S("m_exps", l).at(j + 1))
                    act.wait_ge(*S("m_keys", l).at(j + 1))
                    for u in range(MU):
                        last = fn(mA[:, u, :], psf[:, u * P:(u + 1) * P], ACT.Copy, scale=ex_c[:, 2, u:u + 1])
                    last.then_inc(*S("m_kw", l).by(1))
                    if outs:
                        for d in range(2):
                            c = 2 * count_outs(l, fwd, j) + d
                            act.wait_ge(*S("m_mm", l).at(c + 1))
                            for q in range(MH):
                                u, o = d * MH + q, q % 2 * MV
                                last = fn(mC[:, u, :], ps[:, 6 + q // 2, o:o + MV], ACT.Copy, scale=ex_c[:, 0, u:u + 1])
                            last.then_inc(*S("m_carried", l).by(1))
                st.leave()
                for g in range(2 * full):
                    half, t = g // full, g % full
                    if t < full - 1:
                        act.wait_ge(*S("o_mm", l).at(half * (full - 1) + t + 1))
                    else:
                        act.wait_ge(ring_used, l * LAYER_BLOCKS + B_IN + S_O + half + 1)
                    if g >= 2:
                        act.wait_ge(*S("o_gated", l).at(g - 1))
                    fn(sig_o[:, g % 2, :], ps[:, g % 2, 0:QC], ACT.Sigmoid).then_inc(*S("o_sig", l).by(1))
                    if t == full - 1:
                        split.mixers_to(l, S_O + half + 3)
                st.leave()
                pa = merge_parts(l)
                g = 0
                for it in range(2 * NBR):
                    for j in range(FB):
                        act.wait_ge(*pa.of(*gate_part(it, j)))
                        if g >= 2:
                            act.wait_ge(*S("z_part", l).at(g - 1))
                        col = it // NBR * FB + j
                        bank, bcol = 4 * (g % 2), mgate_b[:, BRANCHES[it % NBR], col:col + 1]
                        if ctx_out:
                            last = fn(even(mg_s[:, g % 2, :]), ps[:, bank:bank + 2, 0:TOK // 2], ACT.Sigmoid, bias=bcol)
                        else:
                            last = fn(mg_s[:, g % 2, 0:LAT], ps[:, bank, :], ACT.Sigmoid, bias=bcol)
                        last.then_inc(*S("z_gate", l).by(1))
                        if j % 2:
                            split.mixers_to(l, S_MERGE + 2 * it + j // 2 + 3)
                        g += 1
                st.leave()
                for t in range(full + 1):
                    if t:
                        u = t - 1
                        act.wait_ge(*S("xn", l).at(u + 1))
                        fn(xn_hi[:, u, :], xnt[:, u % 2, :], ACT.Copy).then_inc(*S("xn_hi", l).by(1))
                        act.wait_ge(*S("xn_T", l).at(u + 1))
                        if u >= 2:
                            act.wait_ge(*S("r_logits", l).at(u - 1))
                        modulate(h2t[:, u % 2, :, :], u, 2 * D, 2, S("h2_tmp", l))
                    if t < full:
                        for v in range(2):
                            act.wait_ge(*S("p_var", l).at(2 * t + v + 1))
                            fn(stat[:, v, 15:16], stat[:, v, 14:15], ACT.Sqrt).then_inc(*S("p_std", l).by(1))
                st.leave()
                act.wait_ge(*S("r_cent", l).at(1))
                fn(aff[:, 0:full, :], aff[:, 0:full, :], ACT.Exp).then_inc(*S("r_exp", l).by(1))
                st.leave()
                g = 0
                for k in range(KD):
                    for grp in range(3 if ctx_out else 2):
                        act.wait_ge(*S("g_mm", l).at(g + 1))
                        s = grp // 2
                        dst = xgT[:, k, 8 * grp:8 * grp + 8, 0:CAPL] if grp < 2 else xgT[:, k, :, CAPL:CAP]
                        fn(dst, ps[:, g % 4, :].rearrange("p (e c) -> p e c", e=E if s else 8), ACT.Identity,
                           bias=modc[:, 2, k, s:s + 1], scale=modc[:, 3, k, s:s + 1]).then_inc(*S("g_out", l).by(1))
                        g += 1
                st.leave()
                m = CAP if ctx_out else CAPL
                r0 = l * LAYER_BLOCKS + B_EXP
                h0 = l * (MIX_SPLITS + EXP_BLOCKS * E) + MIX_SPLITS
                body = 2 * EXP_BLOCKS

                def hi(i, s):
                    act.wait_ge(ring_in[(r0 + s) % RING], i * (16 * body // RING) + 16 * ((r0 + s) // RING + 1))
                    act.wait_ge(ring_used, i * body + (r0 + s - 2))
                    src = raw[:, (r0 + s) % RING, :].rearrange("p (k n) -> p k n", k=4)
                    fn(expert_part(s, 0), src, ACT.Copy).then_inc(S("split_h"), 1)

                def turn(i, final):
                    for s in range(body):
                        j, b = s // EXP_BLOCKS, s % EXP_BLOCKS
                        if s + 2 < body or not final:
                            hi(i, s + 2)
                        if b in (1, 5):
                            act.wait_ge(ring_used, i * body + (r0 + s + 1))
                            c = slice(b // 4 * NCH, (b // 4 + 1) * NCH)
                            fn(hid[0:CAP, c], ps[0:CAP, b // 2, :], ACT.Silu).then_inc(*S("e_sil", l).by(1))
                        if b in (6, 9):
                            half = b // 9
                            act.wait_ge(*S("e_turned", l).at(i * 4 + (2 * j + half + 1)))
                            fn(hd_hi[:, 4 * half:4 * half + 4, :],
                               ps[:, (4, 7)[half], 0:4 * CAP].rearrange("p (k c) -> p k c", k=4), ACT.Copy
                               ).then_inc(*S("e_hH", l).by(1))
                        if b >= 10:
                            half = b - 10
                            act.wait_ge(ring_used, i * body + (r0 + s + 1))
                            act.wait_ge(*S("e_put", l).at(i * 2 + (j + 2)))
                            act.wait_ge(*S("e_comb", l).at(i * 4 * full + (2 * full * (j + 1) + 1)))
                            fn(y_hi[0:m, half * NCH:(half + 1) * NCH], ps[0:m, 5 + half, :], ACT.Copy,
                               scale=val[0:m, 0:1]).then_inc(*S("e_yH", l).by(1))

                hi(0, 0)
                hi(0, 1)
                with turns(act, E // 2 - 1) as i:
                    turn(i, False)
                turn(E // 2 - 1, True)
                st.leave()
                for t in range(full):
                    act.wait_ge(*S("q_var", l).at(t + 1))
                    fn(stat[:, 0, 15:16], stat[:, 0, 14:15], ACT.Sqrt).then_inc(*S("q_std", l).by(1))
                st.leave()

            @block.vector
            def _(dve):
                st = state.setdefault("dve", Stages(dve))
                V = nc.vector
                own = state.setdefault("dve_own", Chain(dve, S("dve_own")))
                if l == 0:
                    dve.drain().then_inc(S("split_v"), RING)

                full = tiles_out(l)
                ctx_out = full == NT
                nt = full * P
                r0 = l * LAYER_BLOCKS

                def even(v):
                    return v.rearrange("p (a n) -> p a n", a=2)

                def result(bank, v):
                    if ctx_out:
                        return ps[:, bank:bank + 2, 0:TOK // 2], even(v)
                    return ps[:, bank, :], v[:, 0:LAT]

                def standardise(src, dst, sf, var, std, count):
                    for half in range(2):
                        own(V.bn_stats(sf[:, 6 * half:6 * half + 6], src[:, half * 512:(half + 1) * 512]))
                    own.wait()
                    own(V.bn_aggr(sf[:, 12:14], sf[:, 0:12]))
                    own.wait()
                    V.tensor_scalar(sf[:, 14:15], sf[:, 13:14], EPS, None, ALU.add).then_inc(*var.by(1))
                    dve.wait_ge(*std.at(count))
                    own(V.reciprocal(sf[:, 16:17], sf[:, 15:16]))
                    own.wait()
                    return V.tensor_scalar(dst, src, sf[:, 12:13], sf[:, 16:17], ALU.subtract, ALU.mult)

                dve.wait_ge(*S("mod_bias_in", l).at(16))
                for c in range(MOD_BLOCKS):
                    dve.wait_ge(ring_used, r0 + c + 1)
                    V.tensor_tensor(mod_row[0:2, c * QC:(c + 1) * QC], ps[0:2, c % 2, 0:QC],
                                    mod_bias[0:2, c * QC:(c + 1) * QC], ALU.add).then_inc(*S("mod_row", l).by(1))
                dve.wait_ge(*S("mod_cols", l).at(1))
                for v in range(4):
                    src = ps[:, 2, v * 2 * KD:(v + 1) * 2 * KD].rearrange("p (k s) -> p k s", k=KD)
                    V.tensor_scalar(modc[:, v, :, :], src, float(v % 2), None, ALU.add)
                st.leave()
                for t in range(NT + 1):
                    if t < NT:
                        dve.wait_ge(*S(f"x_in{t % 2}", l).at(16 * (t // 2 + 1)))
                        if t >= 2:
                            dve.wait_ge(*S("xhat_T", l).at(t - 1))
                        standardise(xin[:, t % 2, :], xhat[:, t % 2, :], stat[:, t % 2, :], S("var", l), S("std", l), t + 1
                                    ).then_inc(*S("xhat", l).by(1))
                    if t:
                        u = t - 1
                        dve.wait_ge(*S("h_hi", l).at(u + 1))
                        c = slice(u * P, (u + 1) * P)
                        V.tensor_tensor(h_lo[:, :, c], htmp[:, u % 2, :, :], h_hi[:, :, c].bitcast(f32), ALU.subtract
                                        ).then_inc(*S("h_done", l).by(1))
                st.leave()
                st.leave()
                dve.wait_ge(*S("rope_in", l).at(32))
                for j in range(6):
                    q = y_v[0][:, j, 0:LAT] if j < FB else kA[:, j - FB, 0:LAT]
                    dve.wait_ge(*S("rope_rot", l).at(j + 1))
                    V.tensor_tensor(rope_s[:, j % 2, :], ps[:, j % 2, :], rope_t[:, 1, :], ALU.mult).then_inc(*S("rope_done", l).by(1))
                    own(V.tensor_tensor(q, q, rope_t[:, 0, :], ALU.mult))
                    own.wait()
                    dve.wait_ge(*S("rope_done", l).at(j + 1))
                    V.tensor_tensor(q, q, rope_s[:, j % 2, :], ALU.add)
                st.leave()
                us = units(l)
                for s in range(len(us) + VLAG):
                    if s < len(us):
                        kind, h, t = us[s]
                        lo, hi = local_keys(kind, t)
                        nl = hi - lo
                        sf, b = soft[:, s % NSOFT, :], 2 * (s % 2)
                        dve.wait_ge(*S("a_scores", l).at(s + 1))
                        if s >= NPROB:
                            dve.wait_ge(*S("a_turned", l).at(s - NPROB + 1))
                        if kind == "B" and t == 0:
                            dve.wait_ge(*S(f"bias_in{h % 2}", l).at(16 * (h // 2 + 1)))
                        if nl and kind == "A":
                            o = P if t == 0 else 0
                            own(V.tensor_tensor(prob[:, s % NPROB, 0:nl], ps[:, b, 0:nl], band[:, o:o + nl], ALU.add))
                        elif nl:
                            o = (LAT // GRID_W - 1 - 2 * t) * GRID_W
                            own(V.tensor_tensor(prob[:, s % NPROB, 0:nl], ps[:, b, 0:nl], bias[:, h % 2, o:o + nl], ALU.add))
                        own(V.tensor_reduce(sf[:, 1:2], ps[:, b + 1, 0:CTX], AX, ALU.max))
                        if nl:
                            own.wait(1)
                            own(V.tensor_reduce(sf[:, 0:1], prob[:, s % NPROB, 0:nl], AX, ALU.max))
                        own.wait()
                        first = sf[:, 0:1] if nl else sf[:, 1:2]
                        second = sink_b[:, h:h + 1] if kind == "A" else first
                        own(V.tensor_scalar(sf[:, 7:8], sf[:, 1:2], first, second, ALU.max, ALU.max))
                        own.wait()
                        V.tensor_scalar(sf[:, 2:3], sf[:, 7:8], -1.0, None, ALU.mult).then_inc(*S("a_max", l).by(1))
                    if 1 <= s <= len(us):
                        u = s - 1
                        kind, h, t = us[u]
                        lo, hi = local_keys(kind, t)
                        sf = soft[:, u % NSOFT, :]
                        dve.wait_ge(*S("a_exp", l).at(u + 1))
                        total = sf[:, 4:5]
                        if hi > lo and kind == "A":
                            own(V.tensor_scalar(sf[:, 7:8], total, sf[:, 3:4], sf[:, 5:6], ALU.add, ALU.add))
                        elif hi > lo or kind == "A":
                            own(V.tensor_scalar(sf[:, 7:8], total, sf[:, 3:4] if hi > lo else sf[:, 5:6], None, ALU.add))
                        if hi > lo or kind == "A":
                            own.wait()
                            total = sf[:, 7:8]
                        V.reciprocal(sf[:, 6:7], total).then_inc(*S("a_rcp", l).by(1))
                    if s >= VLAG:
                        u = s - VLAG
                        kind, h, t = us[u]
                        hp = h % 2 * HD
                        dve.wait_ge(*S("a_values", l).at(u + 1))
                        V.tensor_copy(y_v["AB".index(kind)][hp:hp + HD, h // 2, t * P:(t + 1) * P], ps[0:HD, 6 + u % 2, 0:P]
                                      ).then_inc(*S("a_out", l).by(1))
                st.leave()
                dve.wait_ge(*S("conv_zero", l).at(1))
                for j in range(FB):
                    dve.wait_ge(*S("conv_sig", l).at(j + 1))
                    b = 4 * (j % 2)
                    last = V.tensor_tensor(cpad[:, j, HALO:HALO + LAT], ps[:, b, :], csg[:, 0:LAT], ALU.mult)
                    if ctx_out:
                        last = V.tensor_tensor(cpad[:, j, LSEG + HALO:LSEG + HALO + CTX], ps[:, b + 1, 0:CTX],
                                               csg[:, LAT:TOK], ALU.mult)
                    last.then_inc(*S("conv_glu", l).by(1))
                st.leave()
                for d in range(2):
                    c = slice(d * MH, (d + 1) * MH)
                    for x, o in ((ig_c, 8 * d), (lf_c, 8 * d + 4)):
                        own(V.tensor_tensor(x[:, :, c], gates[:, :, o:o + MH],
                                            gate_b[:, o:o + MH].unsqueeze(1).to_broadcast([P, NT, MH]), ALU.add))
                own(V.memset(vD[:, :, :, P:MV], 1.0))
                own.wait()
                V.scalar_tensor_tensor(lt_c[:, :, :], lf_c[:, :, :], -1.0, lf_c[:, :, :], ALU.mult, ALU.max
                                       ).then_inc(*S("m_abs", l).by(1))
                dve.wait_ge(*S("m_log", l).at(1))
                V.scalar_tensor_tensor(lf_c[:, :, :], lf_c[:, :, :], 0.0, lt_c[:, :, :], ALU.min, ALU.subtract)
                segs = [(0, 0, LAT), (LSEG, LAT, CTX)] if ctx_out else [(0, 0, LAT)]
                for tap in range(KS):
                    for j in range(FB):
                        for src, dst, size in segs:
                            y = y_v[2][:, j, dst:dst + size]
                            x = cpad[:, j, src + tap:src + tap + size]
                            if tap == 0:
                                own(V.tensor_scalar(y, x, conv_c[:, j, 0:1], conv_c[:, j, KS:KS + 1], ALU.mult, ALU.add))
                            else:
                                own.wait(FB * len(segs) - 1)
                                own(V.scalar_tensor_tensor(y, x, conv_c[:, j, tap:tap + 1], y, ALU.mult, ALU.add))
                st.leave()
                dve.wait_ge(*S("conv_sum", l).at(1))
                for j in range(FB):
                    p_, y = result(2, y_v[2][:, j, :])
                    V.scalar_tensor_tensor(y, p_, -1.0 / BW, y, ALU.mult, ALU.add).then_inc(*S("conv_cent", l).by(1))
                dve.wait_ge(*S("conv_sumsq", l).at(FB))
                p_, y = result(4, cstd)
                V.tensor_scalar(y, p_, 1.0 / BW, EPS, ALU.mult, ALU.add).then_inc(*S("conv_var", l).by(1))
                dve.wait_ge(*S("conv_std", l).at(1))
                own(V.reciprocal(cstd[:, 0:nt], cstd[:, 0:nt]))
                own.wait()
                dve.wait_ge(*S("conv_cent", l).at(FB))
                for j in range(FB):
                    V.tensor_tensor(y_v[2][:, j, 0:nt], y_v[2][:, j, 0:nt], cstd[:, 0:nt], ALU.mult
                                    ).then_inc(*S("conv_normed", l).by(1))
                st.leave()
                fwd, bwd = [4, 5, 0, 1, 2, 3], [5, 4, 3, 2, 1, 0]
                own(V.memset(cst, 0.0))
                own(V.memset(m_c, 0.0))
                own(V.memset(hD, 0.0))
                dve.wait_ge(*S("m_cum", l).at(1))
                for d in range(2):
                    c = slice(d * MH, (d + 1) * MH)
                    F = ps[:, 0, d * NT * MH:(d + 1) * NT * MH].rearrange("p (t m) -> p t m", t=NT)
                    own(V.tensor_tensor(u_c[:, :, c], ig_c[:, :, c], F, ALU.subtract))
                    own(V.tensor_copy(F_c[:, :, c], F))
                own(V.tensor_copy(FL_c[:, :, :], ps[:, 1, 0:NT * MU].rearrange("p (t m) -> p t m", t=NT)))
                own.wait()
                idb = ident.unsqueeze(1).to_broadcast([P, MH, P])
                for j in range(NT):
                    chunk = (fwd[j], bwd[j])
                    outs = fwd[j] < full
                    io = count_outs(l, fwd, j)
                    dirs = [(d, slice(d * MH, (d + 1) * MH)) for d in range(2)]

                    def diagonal(col):
                        own(V.tensor_tensor(mA[:, 0:MH, :], idb, col(0).unsqueeze(2).to_broadcast([P, MH, P]), ALU.mult))
                        V.tensor_tensor(mA[:, MH:MU, :], idb, col(1).unsqueeze(2).to_broadcast([P, MH, P]), ALU.mult
                                        ).then_inc(*S("m_diag", l).by(1))

                    diagonal(lambda d: u_c[:, chunk[d], dirs[d][1]])
                    dve.wait_ge(*S("m_rows", l).at(2 * j + 1))
                    rows = ps[:, 0:2, :].rearrange("p b (q n) -> p (b q) n", q=MH)
                    own(V.tensor_reduce(cm_c[:, 1, :], rows, AX, ALU.max))
                    for d, c in dirs:
                        mask = (neg_le, neg_ge)[d]
                        own(V.tensor_tensor(mB[:, c, :], rows[:, c, :], mask.unsqueeze(1).to_broadcast([P, MH, P]), ALU.add))
                    own.wait()
                    own(V.tensor_reduce(cm_c[:, 0, :], mB, AX, ALU.max))
                    own.wait()
                    for v in range(2):
                        own(V.tensor_tensor(M_c[:, v, :], cm_c[:, v, :], m_c, ALU.max))
                    own.wait()
                    own(V.tensor_scalar(nM_c, M_c[:, 0, :], -1.0, None, ALU.mult))
                    for v in range(2):
                        own(V.tensor_tensor(ex_in[:, v, :], m_c, M_c[:, v, :], ALU.subtract))
                    for d, c in dirs:
                        own(V.tensor_tensor(ex_in[:, 2, c], u_c[:, chunk[d], c], M_c[:, 1, c], ALU.subtract))
                    own.wait()
                    for d, c in dirs:
                        own(V.tensor_tensor(ex_in[:, 3, c], nM_c[:, c], F_c[:, chunk[d], c], ALU.subtract))
                        own(V.tensor_tensor(m_c[:, c], M_c[:, 1, c], FL_c[:, chunk[d], c], ALU.add))
                    own.wait()
                    diagonal(lambda d: nM_c[:, dirs[d][1]])
                    dve.wait_ge(*S("m_rows", l).at(2 * j + 2))
                    for d, c in dirs:
                        mask = (neg_ge, neg_le)[d]
                        ins = V.tensor_tensor(mB[:, c, :], rows[:, c, :], mask.unsqueeze(1).to_broadcast([P, MH, P]), ALU.add)
                        if d:
                            ins.then_inc(*S("m_arg", l).by(1))
                        else:
                            own(ins)
                    if outs:
                        own.wait()
                        dve.wait_ge(*S("m_arg", l).at(j + 1))
                        for d, c in dirs:
                            ins = V.tensor_tensor(mB[:, c, :], mB[:, c, :],
                                                  u_c[:, chunk[d], c].unsqueeze(2).to_broadcast([P, MH, P]), ALU.add)
                            if d:
                                ins.then_inc(*S("m_arg2", l).by(1))
                            else:
                                own(ins)
                        dve.wait_ge(*S("m_gate", l).at(io + 1))
                        dve.wait_ge(*S("m_scores", l).at(io + 1))
                        V.tensor_tensor(mB, mB, ps[:, 2:4, :].rearrange("p b (q n) -> p (b q) n", q=MH), ALU.mult
                                        ).then_inc(*S("m_weights", l).by(1))
                        dve.wait_ge(*S("m_exps", l).at(j + 1))
                        for d, c in dirs:
                            dve.wait_ge(*S("m_carried", l).at(2 * io + d + 1))
                            num = mC[:, c, :].rearrange("p (a b) n -> p a (b n)", a=2)
                            V.tensor_tensor(num, num, ps[:, 4:6, 0:2 * MV], ALU.add).then_inc(*S("m_num", l).by(1))
                            dve.wait_ge(*S("m_num", l).at(2 * io + d + 1))
                            dn = mC[:, c, P:MV].rearrange("p h n -> p (h n)")
                            own(V.scalar_tensor_tensor(den[:, 0, c], dn, -1.0, dn, ALU.mult, ALU.max))
                            own.wait()
                            own(V.tensor_tensor(den[:, 1, c], den[:, 0, c], ex_c[:, 3, c], ALU.max))
                            own.wait()
                            own(V.reciprocal(den[:, 2, c], den[:, 1, c]))
                            own.wait()
                            for q in range(MH):
                                hs = hD[:, chunk[d], q * P:(q + 1) * P]
                                own(V.scalar_tensor_tensor(hs, mC[:, d * MH + q, 0:P], den[:, 2, d * MH + q:d * MH + q + 1], hs,
                                                           ALU.mult, ALU.add))
                    dve.wait_ge(*S("m_exps", l).at(j + 1))
                    for d, c in dirs:
                        dve.wait_ge(*S("m_outer", l).at(2 * j + d + 1))
                        for q in range(MH):
                            u, o = d * MH + q, q % 2 * MV
                            last = V.scalar_tensor_tensor(cst[:, u, :], cst[:, u, :], ex_c[:, 1, u:u + 1],
                                                          ps[:, 2 + q // 2, o:o + MV], ALU.mult, ALU.add)
                            if q < MH - 1:
                                own(last)
                        last.then_inc(*S("m_state", l).by(1))
                    own.wait()
                    dve.wait_ge(*S("m_state", l).at(2 * j + 2))
                st.leave()
                for g in range(2 * full):
                    half, t = g // full, g % full
                    dve.wait_ge(*S("o_sig", l).at(g + 1))
                    c = hD[:, t, half * QC:(half + 1) * QC]
                    V.tensor_tensor(c, c, sig_o[:, g % 2, :], ALU.mult).then_inc(*S("o_gated", l).by(1))
                    dve.wait_ge(*S("o_turned", l).at(g + 1))
                    V.tensor_copy(y_v[3][:, 2 * half:2 * half + 2, t * P:(t + 1) * P],
                                  ps[:, 2 + g % 2, 0:QC].rearrange("p (b n) -> p b n", b=2)).then_inc(*S("o_out", l).by(1))
                st.leave()
                pa = merge_parts(l)
                g = 0
                for it in range(2 * NBR):
                    for j in range(FB):
                        dve.wait_ge(*S("z_gate", l).at(g + 1))
                        dve.wait_ge(*pa.of(B_MERGE + 3 * it + 2, j))
                        p_, s_ = result(4 * (g % 2) + 2, mg_s[:, g % 2, :])
                        z = zT[:, it // NBR * FB + j, :]
                        if it % NBR == 0:
                            V.tensor_tensor(even(z) if ctx_out else z[:, 0:LAT], p_, s_, ALU.mult).then_inc(*S("z_part", l).by(1))
                        else:
                            t_ = mg_t[:, g % 2, :]
                            V.tensor_tensor(even(t_) if ctx_out else t_[:, 0:LAT], p_, s_, ALU.mult
                                            ).then_inc(*S("z_part", l).by(1))
                            dve.wait_ge(*S("z_part", l).at(g + 1))
                            own.wait()
                            own(V.tensor_tensor(z[:, 0:nt], z[:, 0:nt], t_[:, 0:nt], ALU.add))
                        g += 1
                st.leave()
                op = out_parts(l)
                dve.wait_ge(*S("rows1_in", l).at(64))

                def affine(x, row_g, row_b, done):
                    own(V.tensor_tensor(x, x, row_g, ALU.mult))
                    own.wait()
                    done(V.tensor_tensor(x, x, row_b, ALU.add))

                for t in range(full + 1):
                    if t < full:
                        for c in range(4):
                            dve.wait_ge(*op.of(B_OUT + c, t))
                        x, tmp = xt[:, t % 2, :], t1[:, t % 2, :]
                        V.tensor_tensor(tmp, psf[:, t % 2 * D:(t % 2 + 1) * D], rows1[:, t // TL, :], ALU.mult
                                        ).then_inc(*S("p_y", l).by(1))
                        dve.wait_ge(*S("p_y", l).at(t + 1))
                        dve.wait_ge(*S(f"pt_in{t % 2}", l).at(16 * (t // 2 + 1)))
                        own(V.scalar_tensor_tensor(x, x, ALPHA, tmp, ALU.mult, ALU.add))
                        own.wait()
                        own(standardise(x, x, stat[:, 0, :], S("p_var", l), S("p_std", l), 2 * t + 1))
                        own.wait()
                        affine(x, rows1[:, 2, :], rows1[:, 3, :], own)
                        own.wait()
                        if t >= 2:
                            dve.wait_ge(*S("xn_T", l).at(t - 1))
                            dve.wait_ge(*S("xn_lo", l).at(t - 1))
                        standardise(x, xnt[:, t % 2, :], stat[:, 1, :], S("p_var", l), S("p_std", l), 2 * t + 2
                                    ).then_inc(*S("xn", l).by(1))
                    if t:
                        u = t - 1
                        dve.wait_ge(*S("xn_hi", l).at(u + 1))
                        V.tensor_tensor(xn_lo[:, u, :], xnt[:, u % 2, :], xn_hi[:, u, :].bitcast(f32), ALU.subtract
                                        ).then_inc(*S("xn_lo", l).by(1))
                st.leave()
                dve.wait_ge(*S("r_logits", l).at(full))
                lg = ps[:, 6, 0:full * E].rearrange("p (t e) -> p t e", t=full)
                af = aff[:, 0:full, :]

                def over_e(v):
                    return v.unsqueeze(2).to_broadcast([P, full, E])

                own(V.tensor_reduce(rsm[:, 0, 0:full], lg, AX, ALU.max))
                own.wait()
                V.tensor_tensor(af, lg, over_e(rsm[:, 0, 0:full]), ALU.subtract).then_inc(*S("r_cent", l).by(1))
                dve.wait_ge(*S("r_exp", l).at(1))
                own(V.tensor_reduce(rsm[:, 1, 0:full], af, AX, ALU.add))
                own.wait()
                own(V.reciprocal(rsm[:, 2, 0:full], rsm[:, 1, 0:full]))
                own.wait()
                V.tensor_tensor(af, af, over_e(rsm[:, 2, 0:full]), ALU.mult).then_inc(*S("r_aff", l).by(1))
                dve.wait_ge(*S("r_affT", l).at(1))
                own(V.tensor_copy(affR[0:E, 0:nt], psf[0:E, 2 * 512:2 * 512 + nt]))
                own(V.tensor_copy(left[0:E, 0:nt], psf[0:E, 2 * 512:2 * 512 + nt]))
                own.wait()
                for a, b, cap in ((0, LAT, CAPL), (LAT, TOK, CAPC))[:2 if ctx_out else 1]:
                    for _ in range(cap // 8):
                        own(V.max(top8[0:E, :], left[0:E, a:b]))
                        own.wait()
                        own(V.match_replace(left[0:E, a:b], top8[0:E, :], left[0:E, a:b], -1.0))
                        own.wait()
                own(V.tensor_scalar(left[0:E, 0:nt], left[0:E, 0:nt], 0.0, None, ALU.is_lt))
                own.wait()
                for a, b in ((0, LAT), (LAT, TOK))[:2 if ctx_out else 1]:
                    own(V.tensor_tensor_scan(took[0:E, a:b], left[0:E, a:b], left[0:E, a:b], 0.0, ALU.add, ALU.max))
                own.wait()
                own(V.tensor_tensor(took[0:E, 0:nt], took[0:E, 0:nt], left[0:E, 0:nt], ALU.mult))
                own.wait()
                V.tensor_scalar(slotR[0:E, 0:nt], took[0:E, 0:nt], -1.0, None, ALU.add).then_inc(*S("slots", l).by(1))
                dve.wait_ge(*S("r_slotT", l).at(1))
                own(V.tensor_copy(slotT[:, 0:full, :], ps[:, 4, 0:full * E].rearrange("p (t e) -> p t e", t=full)))
                own.wait()
                for t in range(full):
                    if t < TL:
                        cap, picks = CAPL, [(pick_l[g][:, t, :, :], 8 * g, 8) for g in range(2)]
                    else:
                        cap, picks = CAPC, [(pick_c[:, t - TL, :, :], 0, E)]
                    for dst, e0, ne in picks:
                        V.tensor_tensor(dst, slot_row[:, 0:cap].unsqueeze(1).to_broadcast([P, ne, cap]),
                                        slotT[:, t, e0:e0 + ne].unsqueeze(2).to_broadcast([P, ne, cap]), ALU.is_equal)
                st.leave()
                if not ctx_out:
                    V.memset(xgT[:, :, :, CAPL:CAP], 0.0)
                st.leave()
                m = CAP if ctx_out else CAPL
                nload = 4 if ctx_out else 2
                r0e = l * LAYER_BLOCKS + B_EXP
                h0 = l * (MIX_SPLITS + EXP_BLOCKS * E) + MIX_SPLITS
                ncomb = 2 * full
                per = ncomb // 4
                body = 2 * EXP_BLOCKS

                def rest(i, s):
                    dve.wait_ge(S("split_h"), i * body + (h0 + s + 1))
                    src = raw[:, (r0e + s) % RING, :].rearrange("p (k n) -> p k n", k=4)
                    V.tensor_tensor(expert_part(s, 1), src, expert_part(s, 0).bitcast(f32), ALU.subtract
                                    ).then_inc(S("split_v"), 1)

                def add(c, base):
                    dve.wait_ge(*S("e_comb", l).at(base + (c + 2)))
                    a = acc[:, c % full, c // full * NCH:(c // full + 1) * NCH]
                    V.tensor_tensor(a, a, ps[:, (4, 7)[c % 2], :], ALU.add).then_inc(*S("e_acc", l).by(1))

                def turn(i, final):
                    for s in range(body):
                        j, b = s // EXP_BLOCKS, s % EXP_BLOCKS
                        if s + 2 < body or not final:
                            rest(i, s + 2)
                        if b < 4:
                            for c in range(b * per, (b + 1) * per):
                                add(c, i * 2 * ncomb + ncomb * j)
                        if b == 4:
                            dve.wait_ge(*S("pair_in", l).at(i * 32 * nload + 16 * nload * (j + 1)))
                            dve.wait_ge(*S("e_comb", l).at(i * 2 * ncomb + (ncomb * (j + 1) + 1)))
                            for a, z, r in ((0, LAT, slice(0, CAPL)), (LAT, TOK, slice(CAPL, CAP)))[:2 if ctx_out else 1]:
                                V.tensor_scalar(put[r, a:z], pair[r, 0, a:z], slot_col[r, :], None, ALU.is_equal)
                                last = V.scalar_tensor_tensor(vscr[r, a:z], pair[r, 0, a:z], slot_col[r, :], pair[r, 1, a:z],
                                                              ALU.is_equal, ALU.mult, accum_out=val[r, 0:1])
                            last.then_inc(*S("e_put", l).by(1))
                        if b in (3, 7):
                            half = b // 4
                            dve.wait_ge(*S("e_sil", l).at(i * 4 + (2 * j + half + 1)))
                            dve.wait_ge(ring_used, i * body + (r0e + s + 1))
                            c = slice(half * NCH, (half + 1) * NCH)
                            V.tensor_tensor(hid[0:CAP, c], hid[0:CAP, c], ps[0:CAP, 2 * half + 1, :], ALU.mult
                                            ).then_inc(*S("e_hid", l).by(1))
                        if b in (6, 9):
                            half = b // 9
                            dve.wait_ge(*S("e_hH", l).at(i * 4 + (2 * j + half + 1)))
                            c = slice(4 * half, 4 * half + 4)
                            V.tensor_tensor(hd_lo[:, c, :], ps[:, (4, 7)[half], 0:4 * CAP].rearrange("p (k c) -> p k c", k=4),
                                            hd_hi[:, c, :].bitcast(f32), ALU.subtract).then_inc(*S("e_hL", l).by(1))
                        if b >= 10:
                            half = b - 10
                            dve.wait_ge(*S("e_yH", l).at(i * 4 + (2 * j + half + 1)))
                            c = slice(half * NCH, (half + 1) * NCH)
                            V.scalar_tensor_tensor(y_lo[0:m, c], ps[0:m, 5 + half, :], val[0:m, 0:1],
                                                   y_hi[0:m, c].bitcast(f32), ALU.mult, ALU.subtract
                                                   ).then_inc(*S("e_yL", l).by(1))

                for v, cols in ((put, TOK), (y_hi, D), (y_lo, D)):
                    own(V.tensor_scalar(v[0:CAP, :], consts[0:CAP, 0:1].to_broadcast([CAP, cols]), 0.0, None, ALU.mult))
                own.wait()
                dve.drain().then_inc(*S("put_zero", l).by(1))
                dve.wait_ge(*S("acc_zero", l).at(1))
                dve.drain().then_inc(*S("e_put", l).by(1))
                dve.drain().then_inc(*S("e_acc", l).by(1))
                dve.drain().then_inc(*S("e_yL", l).by(2))
                rest(0, 0)
                rest(0, 1)
                with turns(dve, E // 2 - 1) as i:
                    turn(i, False)
                turn(E // 2 - 1, True)
                for c in range(ncomb):
                    add(c, E * ncomb)
                st.leave()
                dve.wait_ge(*S("rows2_in", l).at(64))
                dve.wait_ge(*S("x1_in", l).at(16 * full))
                for t in range(full):
                    x, a = x2v[:, t, :], acc[:, t, :]
                    own(V.tensor_tensor(a, a, rows2[:, t // TL, :], ALU.mult))
                    own.wait()
                    own(V.scalar_tensor_tensor(x, x, ALPHA, a, ALU.mult, ALU.add))
                    own.wait()
                    own(standardise(x, x, stat[:, 0, :], S("q_var", l), S("q_std", l), t + 1))
                    own.wait()
                    affine(x, rows2[:, 2, :], rows2[:, 3, :], lambda ins: ins.then_inc(*S("x2", l).by(1)))
                st.leave()

        for l in range(DEPTH):
            layer(l)
            for sem in sems.values():
                if isinstance(sem, Signal):
                    sem.next_layer()


def count_outs(l, order, j):
    return sum(c < tiles_out(l) for c in order[:j])


_DIRECT = ["x", "ctx", "w_mod", "b_mod", "attn_sink", "mlstm_gate_b", "w_branch", "w_gate", "w_out", "ln1_g", "ln1_b",
           "w_router", "w_exp_gate", "w_exp_up", "w_exp_down", "ln2_g", "ln2_b"]


def _layouts(inputs):
    a = {n: np.ascontiguousarray(inputs[n]) for n in _DIRECT}
    f = np.float32

    def col_major(v):
        return np.moveaxis(v.reshape(v.shape[:-1] + (-1, P)), -1, 0)

    a["cT"] = np.ascontiguousarray(np.stack([col_major(inputs["c"][0]), col_major(inputs["c_ctx"])], axis=-1))
    w = inputs["w_in"]
    o = {"qA": 0, "kA": 512, "vA": 640, "qB": 768, "kB": 1280, "vB": 1792, "ca": 2304, "cg": 2816, "qD": 3328,
         "kD": 3840, "vD": 4352, "oD": 4864, "g": 5376}
    blk = np.zeros((DEPTH, IN_BLOCKS, D, QC), f)
    for i, (name, half) in enumerate([("qA", 0), ("qA", 1), (None, 0), (None, 0), ("qB", 0), ("qB", 1), ("kB", 0), ("kB", 1),
                                      ("vB", 0), ("vB", 1), ("ca", 0), ("cg", 0), ("ca", 1), ("cg", 1), ("qD", 0), ("qD", 1),
                                      ("kD", 0), ("kD", 1), ("vD", 0), ("vD", 1), ("oD", 0), ("oD", 1)]):
        if name:
            blk[:, i] = w[:, :, o[name] + half * QC:o[name] + (half + 1) * QC]
    for r in range(4):
        blk[:, 2, :, r * HD:(r + 1) * HD] = w[:, :, o["kA"] + r // 2 * HD:o["kA"] + (r // 2 + 1) * HD]
    blk[:, 3, :, 0:P] = w[:, :, o["vA"]:o["vA"] + P]
    blk[:, 3, :, P:P + 4 * MH] = w[:, :, o["g"]:o["g"] + 4 * MH]
    a["w_in"] = np.ascontiguousarray(blk.reshape(DEPTH, IN_BLOCKS, KD, P, QC).transpose(0, 1, 3, 2, 4)
                                     .reshape(DEPTH, IN_BLOCKS, P, KD * QC))
    cc = np.concatenate([inputs["conv_w"].transpose(0, 2, 1), inputs["conv_b"][..., None],
                         inputs["conv_ln_g"][..., None], inputs["conv_ln_b"][..., None]], axis=-1)
    a["conv_c"] = np.ascontiguousarray(cc.reshape(DEPTH, FB, P, KS + 3).transpose(0, 2, 1, 3))
    a["b_gate"] = np.ascontiguousarray(inputs["b_gate"].reshape(DEPTH, NBR, KD, P).transpose(0, 3, 1, 2))
    rpb = inputs["na_rpb"]
    nr, ncol = rpb.shape[2], rpb.shape[3]
    reach, win = nr // 2, (ncol + 1) // 2
    bias = np.full((DEPTH, 2, GRID_W, HEADS, DROWS, GRID_W), NEG, f)
    for qc in range(GRID_W):
        c0 = min(max(qc - win // 2, 0), GRID_W - win)
        for par in range(2):
            for r in range(par, min(DROWS, nr + par)):
                bias[:, par, qc, :, r, c0:c0 + win] = rpb[:, :, r - par, c0 - qc + win - 1:c0 - qc + 2 * win - 1]
    a["bias"] = np.ascontiguousarray(bias.reshape(DEPTH, P, HEADS, DROWS * GRID_W))
    i, j = np.arange(P)[:, None], np.arange(P)[None, :]
    a["consts"] = np.concatenate([
        np.eye(P), np.ones((P, P)), i <= j, i >= j,
        np.where(j >= i, 0, NEG), np.zeros((P, P)), np.where(j <= i, 0, NEG)], axis=1).astype(f)
    slot = np.where(np.arange(P) < CAPL, np.arange(P), np.arange(P) - CAPL)
    a["iotas"] = np.concatenate([slot[:, None], np.broadcast_to(np.arange(CAPL), (P, CAPL))], axis=1).astype(f)
    half, nf = HD // 2, HD // 4
    inv = (f(10000.0) ** (-np.arange(nf, dtype=f) / f(nf))).astype(f)
    d = np.arange(P) % HD
    t = np.arange(LAT)
    pos = np.where(d[:, None] < half, t[None] // GRID_W, t[None] % GRID_W).astype(f)
    ang = pos * inv[d % nf][:, None]
    rot = np.zeros((P, P), f)
    for q in range(P):
        rot[q + nf if d[q] % half < nf else q - nf, q] = -1 if d[q] % half < nf else 1
    a["rope"] = np.concatenate([np.cos(ang), np.sin(ang), rot], axis=1).astype(f)
    return a


def kernel(**inputs):
    import concourse.bacc as _bacc
    from concourse.bass_utils import run_bass_kernel_spmd as _run
    inputs = {n: np.asarray(v) for n, v in inputs.items()}
    arrays = _layouts(inputs)
    nc = _bacc.Bacc("TRN2", target_bir_lowering=False, num_devices=1)
    args = {n: nc.dram_tensor(f"in_{n}", v.shape, mybir.dt.from_np(v.dtype), kind="ExternalInput").ap()
            for n, v in arrays.items()}
    out = nc.dram_tensor("out_x", (1, LAT, D), mybir.dt.float32, kind="ExternalOutput").ap()
    build(nc, args, out)
    r = _run(nc, [{f"in_{n}": v for n, v in arrays.items()}], core_ids=[0])
    return r.results[0]["out_x"]
```
